# Optimizing a Trainium2 kernel written in Bass

```python
import math
import jax, jax.numpy as jnp
from jax import lax
import numpy as np

D_MODEL = 2048
BATCH = 1
SEQ = 256
DEPTH = 1
DEC_BATCH = 1
DEC_SEQ = 512
PAST_LEN = 128

MLA_HEADS = 8
Q_LORA = 512
KV_LORA = 256
QK_NOPE = 128
QK_ROPE = 64
QK_HEAD = QK_NOPE + QK_ROPE
V_HEAD = 128
MLA_WIDTH = MLA_HEADS * V_HEAD
ROPE_THETA = 10000.0
Q_BLOCK = 128
GDN_HEADS = 8
GDN_DK = 128
GDN_DV = 128
GDN_WIDTH = GDN_HEADS * GDN_DV
QKV_GDN = 2 * GDN_HEADS * GDN_DK + GDN_HEADS * GDN_DV
CONV_W = 5
CHUNK = 64
MIX_WIDTH = MLA_WIDTH + GDN_WIDTH
SPLITS = (Q_LORA, KV_LORA, QK_ROPE, QKV_GDN, GDN_WIDTH, GDN_HEADS, GDN_HEADS, GDN_HEADS, GDN_HEADS)
IN_COLS = Q_LORA + KV_LORA + QK_ROPE + QKV_GDN + GDN_WIDTH + 4 * GDN_HEADS
N_EXPERTS = 16
EXPERT_FF = 1024
CAPACITY_FACTOR = 2
EPS = 1e-6

kernel_name = "hybrid_mla_gdn_ec_encoder"

def rms_norm(x, g):
    xf = x.astype(jnp.float32)
    y = xf * lax.rsqrt(jnp.mean(xf * xf, axis=-1, keepdims=True) + EPS)
    return (y * g.astype(jnp.float32)).astype(x.dtype)

def l2_normalize(x):
    xf = x.astype(jnp.float32)
    return xf * lax.rsqrt(jnp.sum(xf * xf, axis=-1, keepdims=True) + EPS)

def split_cols(t, sizes):
    out = []
    off = 0
    for s in sizes:
        out.append(t[..., off:off + s])
        off += s
    return out

def apply_rope(x, pos):
    half = QK_ROPE // 2
    inv_freq = ROPE_THETA ** (-jnp.arange(half, dtype=jnp.float32) / half)
    ang = pos.astype(jnp.float32)[:, None] * inv_freq[None, :]
    cos = jnp.cos(ang)[None, :, None, :]
    sin = jnp.sin(ang)[None, :, None, :]
    x1 = x[..., :half].astype(jnp.float32)
    x2 = x[..., half:].astype(jnp.float32)
    return jnp.concatenate([x1 * cos - x2 * sin, x2 * cos + x1 * sin], axis=-1).astype(x.dtype)

def blocked_attention(q, k, v):
    B, H, S, Dq = q.shape
    nb = S // Q_BLOCK
    qb = q.reshape(B, H, nb, Q_BLOCK, Dq).transpose(2, 0, 1, 3, 4)
    scale = QK_HEAD ** -0.5

    def one_block(qi):
        s = jnp.einsum('bhqd,bhkd->bhqk', qi, k).astype(jnp.float32) * scale
        p = jax.nn.softmax(s, axis=-1).astype(v.dtype)
        return jnp.einsum('bhqk,bhkd->bhqd', p, v)

    o = lax.map(one_block, qb)
    return o.transpose(1, 0, 3, 2, 4).reshape(B, S, H * V_HEAD)

def mla_mixer(q_lat, kv_lat, k_rope, q_a_norm_g, w_q_b, kv_a_norm_g, w_kv_b, q_norm_g, k_norm_g):
    B, S, _ = q_lat.shape
    pos = jnp.arange(S)
    q = (rms_norm(q_lat, q_a_norm_g) @ w_q_b).reshape(B, S, MLA_HEADS, QK_HEAD)
    kv = (rms_norm(kv_lat, kv_a_norm_g) @ w_kv_b).reshape(B, S, MLA_HEADS, QK_NOPE + V_HEAD)
    k_nope, v = kv[..., :QK_NOPE], kv[..., QK_NOPE:]
    k = jnp.concatenate([k_nope, jnp.broadcast_to(k_rope[:, :, None, :], (B, S, MLA_HEADS, QK_ROPE))], axis=-1)
    q = rms_norm(q, q_norm_g)
    k = rms_norm(k, k_norm_g)
    q = jnp.concatenate([q[..., :QK_NOPE], apply_rope(q[..., QK_NOPE:], pos)], axis=-1)
    k = jnp.concatenate([k[..., :QK_NOPE], apply_rope(k[..., QK_NOPE:], pos)], axis=-1)
    return blocked_attention(q.transpose(0, 2, 1, 3), k.transpose(0, 2, 1, 3), v.transpose(0, 2, 1, 3))

def centred_depthwise_conv(x, w):
    C = x.shape[-1]
    pad = CONV_W // 2
    return lax.conv_general_dilated(x, w.reshape(CONV_W, 1, C).astype(x.dtype), window_strides=(1,),
                                    padding=[(pad, pad)], dimension_numbers=('NWC', 'WIO', 'NWC'),
                                    feature_group_count=C)

def chunk_gated_delta(q, k, v, g, beta):
    B, S, H, DK = q.shape
    DV = v.shape[-1]
    N = S // CHUNK

    def to_chunks(t):
        return jnp.swapaxes(t.reshape((B, N, CHUNK, H) + t.shape[3:]), 2, 3)

    q = to_chunks(q) * (DK ** -0.5)
    k = to_chunks(k)
    v = to_chunks(v)
    g = to_chunks(g)
    beta = to_chunks(beta)
    gc = jnp.cumsum(g, axis=-1)
    idx = jnp.arange(CHUNK)
    incl = idx[:, None] >= idx[None, :]
    strict = idx[:, None] > idx[None, :]
    decay = jnp.exp(jnp.where(incl, gc[..., :, None] - gc[..., None, :], -jnp.inf))
    kb = k * beta[..., None]
    L = jnp.where(strict, jnp.einsum('bnhid,bnhjd->bnhij', kb, k) * decay, 0.0)
    A = L + jnp.eye(CHUNK, dtype=L.dtype)
    rhs = jnp.concatenate([v * beta[..., None], kb * jnp.exp(gc)[..., None]], axis=-1)
    sol = lax.linalg.triangular_solve(A, rhs, left_side=True, lower=True, unit_diagonal=True)
    u, w = sol[..., :DV], sol[..., DV:]
    intra = jnp.where(incl, jnp.einsum('bnhid,bnhjd->bnhij', q, k) * decay, 0.0)
    q_dec = q * jnp.exp(gc)[..., None]
    g_last = gc[..., -1]
    k_dec = k * jnp.exp(g_last[..., None] - gc)[..., None]

    def step(state, xs):
        q_d, k_d, u_i, w_i, intra_i, gl = xs
        v_new = u_i - jnp.einsum('bhck,bhkv->bhcv', w_i, state)
        o = jnp.einsum('bhck,bhkv->bhcv', q_d, state) + jnp.einsum('bhcj,bhjv->bhcv', intra_i, v_new)
        state = state * jnp.exp(gl)[..., None, None] + jnp.einsum('bhck,bhcv->bhkv', k_d, v_new)
        return state, o

    xs = (jnp.swapaxes(q_dec, 0, 1), jnp.swapaxes(k_dec, 0, 1), jnp.swapaxes(u, 0, 1),
          jnp.swapaxes(w, 0, 1), jnp.swapaxes(intra, 0, 1), jnp.swapaxes(g_last, 0, 1))
    state0 = jnp.zeros((B, H, DK, DV), jnp.float32)
    _, o = lax.scan(step, state0, xs)
    return o.transpose(1, 0, 3, 2, 4).reshape(B, S, H, DV)

def gdn_mixer(qkv, z, a_f, a_b, b_f, b_b, conv_w, a_log_fwd, a_log_bwd, dt_bias_fwd, dt_bias_bwd, gdn_norm_g):
    B, S, _ = qkv.shape
    qkv = jax.nn.silu(centred_depthwise_conv(qkv, conv_w))
    q, k, v = split_cols(qkv, (GDN_HEADS * GDN_DK, GDN_HEADS * GDN_DK, GDN_HEADS * GDN_DV))
    q = l2_normalize(q.reshape(B, S, GDN_HEADS, GDN_DK))
    k = l2_normalize(k.reshape(B, S, GDN_HEADS, GDN_DK))
    v = v.reshape(B, S, GDN_HEADS, GDN_DV).astype(jnp.float32)
    g_f = -jnp.exp(a_log_fwd.astype(jnp.float32)) * jax.nn.softplus(a_f.astype(jnp.float32) + dt_bias_fwd.astype(jnp.float32))
    g_b = -jnp.exp(a_log_bwd.astype(jnp.float32)) * jax.nn.softplus(a_b.astype(jnp.float32) + dt_bias_bwd.astype(jnp.float32))
    beta_f = jax.nn.sigmoid(b_f.astype(jnp.float32))
    beta_b = jax.nn.sigmoid(b_b.astype(jnp.float32))
    o_f = chunk_gated_delta(q, k, v, g_f, beta_f)
    o_b = jnp.flip(chunk_gated_delta(jnp.flip(q, 1), jnp.flip(k, 1), jnp.flip(v, 1),
                                     jnp.flip(g_b, 1), jnp.flip(beta_b, 1)), 1)
    o = o_f + o_b
    o = o * lax.rsqrt(jnp.mean(o * o, axis=-1, keepdims=True) + EPS) * gdn_norm_g.astype(jnp.float32)
    o = o * jax.nn.silu(z.reshape(B, S, GDN_HEADS, GDN_DV).astype(jnp.float32))
    return o.reshape(B, S, GDN_WIDTH).astype(qkv.dtype)

def ec_moe(x, w_router, w_gate, w_up, w_down):
    B, S, D = x.shape
    T = B * S
    C = max(1, CAPACITY_FACTOR * T // N_EXPERTS)
    xt = x.reshape(T, D)
    aff = jax.nn.softmax((xt @ w_router).astype(jnp.float32), axis=-1)
    gates, idx = lax.top_k(aff.T, C)
    xe = xt[idx]
    h = jax.nn.silu(jnp.einsum('ecd,edf->ecf', xe, w_gate)) * jnp.einsum('ecd,edf->ecf', xe, w_up)
    ye = jnp.einsum('ecf,efd->ecd', h, w_down) * gates[..., None].astype(x.dtype)
    out = jnp.zeros_like(xt).at[idx.reshape(-1)].add(ye.reshape(-1, D))
    return out.reshape(B, S, D)

def encoder_layer(x, norm1_g, w_in, q_a_norm_g, w_q_b, kv_a_norm_g, w_kv_b, q_norm_g, k_norm_g,
                  conv_w, a_log_fwd, a_log_bwd, dt_bias_fwd, dt_bias_bwd, gdn_norm_g, w_o,
                  norm2_g, w_router, w_gate, w_up, w_down):
    h = rms_norm(x, norm1_g)
    proj = h @ w_in
    q_lat, kv_lat, k_rope, qkv, z, a_f, a_b, b_f, b_b = split_cols(proj, SPLITS)
    mla_out = mla_mixer(q_lat, kv_lat, k_rope, q_a_norm_g, w_q_b, kv_a_norm_g, w_kv_b, q_norm_g, k_norm_g)
    gdn_out = gdn_mixer(qkv, z, a_f, a_b, b_f, b_b, conv_w, a_log_fwd, a_log_bwd,
                        dt_bias_fwd, dt_bias_bwd, gdn_norm_g)
    x = x + jnp.concatenate([mla_out, gdn_out], axis=-1) @ w_o
    x = x + ec_moe(rms_norm(x, norm2_g), w_router, w_gate, w_up, w_down)
    return x

def setup_inputs(seed: int = 0) -> dict:
    key = jax.random.key(seed)
    ks = jax.random.split(key, 24)
    f32 = jnp.float32

    def nrm(k, shape, scale):
        return jax.random.normal(k, shape, f32) * scale

    def gain(k, n):
        return 1.0 + 0.02 * jax.random.normal(k, (DEPTH, n), f32)

    dt = jnp.exp(jax.random.uniform(ks[12], (2, DEPTH, GDN_HEADS), f32, math.log(1e-3), math.log(1e-1)))
    dt_bias = dt + jnp.log(-jnp.expm1(-dt))
    a_log = jnp.log(jax.random.uniform(ks[13], (2, DEPTH, GDN_HEADS), f32, 1.0, 16.0))
    return {
        "x_prompt": jax.random.normal(ks[0], (BATCH, SEQ, D_MODEL), f32),
        "x_sample": jax.random.normal(ks[1], (DEC_BATCH, DEC_SEQ, D_MODEL), f32),
        "norm1_g": gain(ks[2], D_MODEL),
        "w_in": nrm(ks[3], (DEPTH, D_MODEL, IN_COLS), D_MODEL ** -0.5),
        "q_a_norm_g": gain(ks[4], Q_LORA),
        "w_q_b": nrm(ks[5], (DEPTH, Q_LORA, MLA_HEADS * QK_HEAD), Q_LORA ** -0.5),
        "kv_a_norm_g": gain(ks[6], KV_LORA),
        "w_kv_b": nrm(ks[7], (DEPTH, KV_LORA, MLA_HEADS * (QK_NOPE + V_HEAD)), KV_LORA ** -0.5),
        "q_norm_g": gain(ks[8], QK_HEAD),
        "k_norm_g": gain(ks[9], QK_HEAD),
        "conv_w": nrm(ks[10], (DEPTH, CONV_W, QKV_GDN), CONV_W ** -0.5),
        "a_log_fwd": a_log[0],
        "a_log_bwd": a_log[1],
        "dt_bias_fwd": dt_bias[0],
        "dt_bias_bwd": dt_bias[1],
        "gdn_norm_g": gain(ks[11], GDN_DV),
        "w_o": nrm(ks[14], (DEPTH, MIX_WIDTH, D_MODEL), MIX_WIDTH ** -0.5),
        "norm2_g": gain(ks[15], D_MODEL),
        "w_router": nrm(ks[16], (DEPTH, D_MODEL, N_EXPERTS), D_MODEL ** -0.5),
        "w_gate": nrm(ks[17], (DEPTH, N_EXPERTS, D_MODEL, EXPERT_FF), D_MODEL ** -0.5),
        "w_up": nrm(ks[18], (DEPTH, N_EXPERTS, D_MODEL, EXPERT_FF), D_MODEL ** -0.5),
        "w_down": nrm(ks[19], (DEPTH, N_EXPERTS, EXPERT_FF, D_MODEL), EXPERT_FF ** -0.5),
    }

def reference(x_prompt, x_sample, norm1_g, w_in, q_a_norm_g, w_q_b, kv_a_norm_g, w_kv_b, q_norm_g,
              k_norm_g, conv_w, a_log_fwd, a_log_bwd, dt_bias_fwd, dt_bias_bwd, gdn_norm_g, w_o,
              norm2_g, w_router, w_gate, w_up, w_down):
    y_prompt = x_prompt
    y_sample = x_sample
    for l in range(DEPTH):
        p = (norm1_g[l], w_in[l], q_a_norm_g[l], w_q_b[l], kv_a_norm_g[l], w_kv_b[l], q_norm_g[l],
             k_norm_g[l], conv_w[l], a_log_fwd[l], a_log_bwd[l], dt_bias_fwd[l], dt_bias_bwd[l],
             gdn_norm_g[l], w_o[l], norm2_g[l], w_router[l], w_gate[l], w_up[l], w_down[l])
        y_prompt = encoder_layer(y_prompt, *p)
        y_sample = encoder_layer(y_sample, *p)
    return (y_prompt, y_sample)


_drawn_inputs = setup_inputs


def setup_inputs(seed=0):
    import zlib

    import numpy as np

    out = dict(_drawn_inputs(seed))
    spreads = {}
    factors = {'norm1_g': 3.309,
     'q_a_norm_g': 8.0,
     'kv_a_norm_g': 8.0,
     'q_norm_g': 8.0,
     'k_norm_g': 8.0,
     'gdn_norm_g': 4.25,
     'norm2_g': 3.691}
    for name, (base, spread) in spreads.items():
        noise = np.random.default_rng([zlib.crc32(name.encode()), seed]).standard_normal(out[name].shape)
        drawn = base * np.exp(spread * noise) if base else spread * noise
        out[name] = __import__('jax').numpy.asarray(drawn.astype(out[name].dtype))
    for name, factor in factors.items():
        out[name] = (out[name] * factor).astype(out[name].dtype)
    return out
```

```python
import math
from contextlib import ExitStack

import numpy as np
import concourse.bass as bass
from concourse import mybir

F32 = mybir.dt.float32
U32 = mybir.dt.uint32
ALU = mybir.AluOpType
ACT = mybir.ActivationFunctionType
AX = mybir.AxisListType.X

P = 128
D = 2048
SP_, SS_ = 256, 512
T = SP_ + SS_
NT = T // P
TILES_P = SP_ // P
KD = D // P
QL, KVL, ROPE, NOPE, VH = 512, 256, 64, 128, 128
QH = NOPE + ROPE
HALF = ROPE // 2
H = 8
HP = H // 2
GW = 1024
C_KV, C_QKV, C_Z, C_AB = QL, QL + KVL + ROPE, QL + KVL + ROPE + 3 * GW, QL + KVL + ROPE + 4 * GW
IN_COLS = C_AB + 4 * H
NKV = KVL + ROPE
NE, FF = 16, 1024
CP, CS = 2 * SP_ // NE, 2 * SS_ // NE
CT = CP + CS
EPS = 1e-6
SEGS = ((0, TILES_P), (TILES_P, NT))
BIG = -1.0e30
TABLES = "natural_log_exp_and_others"
LEVELS = 7


def shape_constants():
    j, i = np.meshgrid(np.arange(P), np.arange(P), indexing="ij")
    parts = [(j == i), (j <= i), (j >= i)]
    parts = [x.astype(np.float32) for x in parts]
    parts += [np.where(i >= j, 0.0, BIG), np.where(i <= j, 0.0, BIG)]
    for lv in range(LEVELS):
        b = 1 << lv
        f = ((j // (2 * b) == i // (2 * b)) & ((j // b) % 2 == 0) & ((i // b) % 2 == 1)).astype(np.float32)
        parts += [f, f.T, f]
    square = np.concatenate([x.astype(np.float32) for x in parts], axis=1)
    inv = (10000.0 ** (-np.arange(HALF, dtype=np.float32) / np.float32(HALF))).astype(np.float32)
    pos = np.concatenate([np.arange(SP_), np.arange(SS_)]).astype(np.float32)
    ang = (pos[:, None] * inv[None, :]).astype(np.float32)
    rope = np.stack([np.cos(ang), np.sin(ang)], axis=1).astype(np.float32)
    rope = rope.reshape(NT, P, 2, HALF).transpose(1, 0, 2, 3)
    return np.ascontiguousarray(square), np.ascontiguousarray(rope)


def build(nc, a, stop_after="moe"):
    ctx = ExitStack()
    with ctx:
        k = Kernel(nc, a, ctx)
        latents(k)
        if stop_after == "latents":
            return
        attention(k)
        if stop_after == "attention":
            return
        deltanet(k)
        if stop_after == "deltanet":
            return
        output_and_route(k)
        if stop_after == "route":
            return
        moe(k)


class Kernel:

    def __init__(self, nc, a, ctx):
        self.nc, self.a, self.ctx = nc, a, ctx
        self.psum = ctx.enter_context(nc.psum_tensor("psum", [P, 8, 512], F32))
        sb = self.sb
        self.passed = ctx.enter_context(nc.semaphore("passed"))
        self.square = sb("square", [P, 5 * P])
        sq = self.square
        self.ident = sq[:, 0:P]
        self.cum = [sq[:, P:2 * P], sq[:, 2 * P:3 * P]]
        self.causal = sq[:, 3 * P:5 * P].rearrange("p (d i) -> p d i", d=2)
        self.mix = nc.dram_tensor("mix", [2 * H, P, T], F32).ap()
        self.x_rows = lambda t: (a["x_prompt"][0, t * P:(t + 1) * P, :] if t < TILES_P
                                 else a["x_sample"][0, (t - TILES_P) * P:(t - TILES_P + 1) * P, :])
        self.y_rows = lambda t: (a["y_prompt"][0, t * P:(t + 1) * P, :] if t < TILES_P
                                 else a["y_sample"][0, (t - TILES_P) * P:(t - TILES_P + 1) * P, :])

    def sb(self, name, shape, dt=F32, ctx=None):
        return (ctx or self.ctx).enter_context(self.nc.sbuf_tensor(name, shape, dt))

    def sem(self, name, ctx=None):
        return (ctx or self.ctx).enter_context(self.nc.semaphore(name))


def bcast(ap, axis, n):
    shape = list(ap.unsqueeze(axis).shape)
    shape[axis] = n
    return ap.unsqueeze(axis).to_broadcast(shape)


def wait_apart(eng, sem, value, k):
    eng.wait_ge(sem, value)
    eng.sem_inc(k.passed, 1)


class Steps:

    def __init__(self, eng, sem, base=0):
        self.eng, self.sem, self.base, self.n = eng, sem, base, 0

    def done(self, ins):
        ins.then_inc(self.sem, 1)
        self.n += 1
        return ins

    def settle(self):
        self.eng.wait_ge(self.sem, self.base + self.n)


def latents(k):
    nc, a, ps = k.nc, k.a, k.psum
    L = k.ctx.enter_context(ExitStack())
    k.gdn_ctx = L
    sb = lambda n, s: k.sb(n, s, ctx=L)
    k.xT = xT = sb("xT", [P, KD, T])
    k.zs = nc.dram_tensor("z_gate", [NT, P, GW], F32).ap()
    k.g_col = g_col = sb("g_col", [P, 96])
    k.b_col = b_col = sb("b_col", [P, 96])
    k.convT = convT = sb("convT", [P, 5 * 24])
    k.rows = nc.dram_tensor("gate_rows", [2, NT, H, 2, P], F32).ap()
    M = k.mla_ctx = L.enter_context(ExitStack())
    sm = lambda n, s: k.sb(n, s, ctx=M)
    k.qlT = qlT = sm("qlT", [P, 4, T])
    k.kvlT = kvlT = sm("kvlT", [P, 2, T])
    k.krope = krope = sm("krope", [P, NT, ROPE])
    k.rope = sm("rope", [P, NT, 2, HALF])

    GROUPS = [(0, QL), (C_KV, NKV), (C_Z, 512), (C_Z + 512, 512)]
    with ExitStack() as c:
        sb = lambda n, s: k.sb(n, s, ctx=c)
        sem = lambda n: k.sem(n, c)
        zs = sb("zs", [P, NT, GW])
        zflat = zs[:].rearrange("p t c -> p (t c)")
        xin = zflat[:, 0:2 * D].rearrange("p (b d) -> p b d", b=2)
        xs = [zflat[:, 2 * D:3 * D], sb("xs1", [P, D])]
        junk = sb("junk", [P, D])
        wb = [sb("wb0", [P, KD, 512]), sb("wb1", [P, KD, 512])]
        ss = sb("ss", [P, 24])
        rs = sb("rs", [P, 24])
        ql = sb("ql", [P, 2, QL])
        abr = sb("abr", [P, 2, 16, NT])
        n1g = sb("n1g", [P, KD])
        qag = sb("qag", [P, 4])
        kvg = sb("kvg", [P, 2])
        gng = sb("gng", [P, P])
        alog = sb("alog", [P, 16])
        dtb = sb("dtb", [P, 16])
        gt = sb("gt", [P, 6, 96])
        rowsb = sb("rowsb", [96, 2, P])
        convr = sb("convr", [120, P])
        eps_sb = sb("eps_sb", [P, 1])

        s_x = [sem("x_loaded0"), sem("x_loaded1")]
        s_w = [sem("w_loaded0"), sem("w_loaded1")]
        s_const = sem("constants_loaded")
        s_xs = sem("x_scaled")
        s_xtp = sem("x_transposed")
        s_xt = sem("xT_stored")
        s_acc = sem("projection_done")
        s_lat = sem("latent_read")
        s_qs = sem("latent_scaled")
        s_qtp = sem("latent_transposed")
        s_qt = sem("latent_stored")
        s_ez = sem("z_silu")
        s_z = sem("z_gated")
        s_eps = sem("eps_set")
        s_act = sem("scalar_step")
        s_vec = sem("vector_step")
        s_ga = sem("gate_scalar")
        s_gv = sem("gate_vector")
        s_gp = sem("gate_tensor")
        s_cv = sem("conv_taps")
        s_rows = sem("rows_stored")

        k.phase = block_ctx = nc.Block()
        with block_ctx as block:
            @block.sync
            def _(sp):
                sp.dma_start(k.square[:], a["square"][:, 0:5 * P]).then_inc(s_const, 16)
                sp.dma_start(n1g[:], a["norm1_g"].rearrange("o (p k) -> p (o k)", k=KD)).then_inc(s_const, 16)

                def load_x(t):
                    if t >= 2:
                        sp.wait_ge(s_xs, t - 1)
                    sp.dma_start(xin[:, t % 2, :], k.x_rows(t)).then_inc(s_x[t % 2], 16)

                def load_w(g):
                    if g >= 2:
                        sp.wait_ge(s_acc, NT * (g - 1))
                    c0, n = GROUPS[g]
                    m = 1
                    w = a["w_in"][0].rearrange("(p k) n -> p k n", k=KD)
                    if g == 1:
                        sp.dma_start(wb[1][:, :, NKV:NKV + 32], w[:, :, C_AB:IN_COLS]).then_inc(s_w[1], 16)
                    sp.dma_start(wb[g % 2][:, :, 0:n], w[:, :, c0:c0 + n]).then_inc(s_w[g % 2], 16)

                load_x(0)
                load_x(1)
                load_w(0)
                sp.dma_start(qag[:], a["q_a_norm_g"].rearrange("o (p k) -> p (o k)", k=4)).then_inc(s_const, 16)
                sp.dma_start(kvg[:], a["kv_a_norm_g"].rearrange("o (p k) -> p (o k)", k=2)).then_inc(s_const, 16)
                sp.dma_start(gng[:], a["gdn_norm_g"][0].partition_broadcast(P)).then_inc(s_const, 16)
                sp.dma_start(alog[:, 0:8], a["a_log_fwd"][0].partition_broadcast(P)).then_inc(s_const, 16)
                sp.dma_start(alog[:, 8:16], a["a_log_bwd"][0].partition_broadcast(P)).then_inc(s_const, 16)
                sp.dma_start(dtb[:, 0:8], a["dt_bias_fwd"][0].partition_broadcast(P)).then_inc(s_const, 16)
                sp.dma_start(dtb[:, 8:16], a["dt_bias_bwd"][0].partition_broadcast(P)).then_inc(s_const, 16)
                sp.dma_start(convr[:], a["conv_w"][0].rearrange("w (n c) -> (w n) c", c=P)).then_inc(s_const, 16)
                sp.dma_start(k.rope[:], a["rope"]).then_inc(s_const, 16)
                for t in range(2, NT):
                    load_x(t)
                for g in range(1, 4):
                    load_w(g)
                sp.wait_ge(s_gv, 6)
                for d in range(2):
                    for h in range(H):
                        r0 = (d * H + h) * NT
                        sp.dma_start(k.rows[d, :, h], rowsb[r0:r0 + NT]).then_inc(s_rows, 16)
                for half in range(2):
                    sp.wait_ge(s_z, NT * (half + 1))
                    sp.dma_start(k.zs[:, :, 512 * half:512 * half + 512].rearrange("t p c -> p t c"),
                                 zs[:, :, 512 * half:512 * half + 512]).then_inc(s_rows, 16)
                sp.wait_ge(s_rows, 16 * (2 * H + 2))

            NCONST = 16 * 11

            @block.scalar
            def _(act):
                st = Steps(act, s_act)
                act.preload_act_table_set(TABLES)
                act.wait_ge(s_eps, 1)

                def rstd(u, n):
                    st.settle()
                    st.done(nc.scalar.activation(ss[:, u:u + 1], ss[:, u:u + 1], ACT.Ln, bias=eps_sb[:], scale=1.0 / n))
                    st.settle()
                    st.done(nc.scalar.activation(rs[:, u:u + 1], ss[:, u:u + 1], ACT.Exp, scale=-0.5))
                    st.settle()

                def scale_x(t):
                    act.wait_ge(s_x[t % 2], 16 * (t // 2 + 1))
                    st.settle()
                    st.done(nc.scalar.activation(junk[:], xin[:, t % 2, :], ACT.Square, accum_out=ss[:, t:t + 1]))
                    rstd(t, D)
                    if t >= 2:
                        act.wait_ge(s_xtp, 4 * (t - 1))
                    nc.scalar.activation(xs[t % 2][:, :], xin[:, t % 2, :], ACT.Copy, scale=rs[:, t:t + 1]).then_inc(s_xs, 1)

                def latent(u, n):
                    acc = ps[:, u % 3, :]
                    act.wait_ge(s_acc, u + 1)
                    st.settle()
                    st.done(nc.scalar.activation(junk[:, 0:n], acc[:, 0:n], ACT.Square, accum_out=ss[:, 6 + u:7 + u]))
                    rstd(6 + u, n)
                    if u >= 2:
                        act.wait_ge(s_qtp, u - 1)
                    if u < NT:
                        nc.scalar.activation(ql[:, u % 2, 0:n], acc[:, 0:n], ACT.Copy,
                                             scale=rs[:, 6 + u:7 + u]).then_inc(s_qs, 1)
                        return
                    t = u - NT
                    nc.scalar.activation(ql[:, u % 2, 0:n], acc[:, 0:n], ACT.Copy,
                                         scale=rs[:, 6 + u:7 + u]).then_inc(s_qs, 1)
                    nc.scalar.copy(krope[:, t, :], acc[:, KVL:NKV])
                    nc.scalar.copy(abr[:, :, :, t], acc[:, NKV:NKV + 32].rearrange("p (k x) -> p k x", k=2)).then_inc(s_lat, 1)

                scale_x(0)
                for t in range(NT):
                    if t + 1 < NT:
                        scale_x(t + 1)
                    latent(t, QL)
                for t in range(NT):
                    latent(NT + t, KVL)
                act.wait_ge(s_gv, 1)
                act.wait_ge(s_lat, NT)
                nc.scalar.activation(gt[:, 1, :], gt[:, 1, :], ACT.Exp, scale=-1.0).then_inc(s_ga, 1)
                nc.scalar.activation(gt[:, 3, :], abr[:, 1].rearrange("p x t -> p (x t)"), ACT.Exp, scale=-1.0).then_inc(s_ga, 1)
                act.wait_ge(s_const, NCONST)
                nc.scalar.activation(alog[:], alog[:], ACT.Exp).then_inc(s_ga, 1)
                act.wait_ge(s_ga, 1)
                nc.scalar.activation(gt[:, 1, :], gt[:, 1, :], ACT.Ln, bias=1.0).then_inc(s_ga, 1)
                for v in range(2 * NT):
                    u, t, half = v + 2 * NT, v % NT, v // NT
                    act.wait_ge(s_acc, u + 1)
                    nc.scalar.activation(zs[:, t, 512 * half:512 * half + 512], ps[:, u % 3, :], ACT.Silu).then_inc(s_ez, 1)

            @block.vector
            def _(dve):
                st = Steps(dve, s_vec)
                nc.vector.memset(eps_sb[:], EPS).then_inc(s_eps, 1)
                dve.wait_ge(s_const, NCONST)

                def store_x(t):
                    for b in range(4):
                        dve.wait_ge(s_xtp, 4 * t + b + 1)
                        nc.vector.tensor_tensor(xT[:, 4 * b:4 * b + 4, t * P:(t + 1) * P],
                                                ps[:, 3 + b, :].rearrange("p (k c) -> p k c", k=4),
                                                bcast(n1g[:, 4 * b:4 * b + 4], 2, P), ALU.mult).then_inc(s_xt, 1)

                def store_latent(u):
                    n, gain, dst, t = (4, qag, qlT, u) if u < NT else (2, kvg, kvlT, u - NT)
                    dve.wait_ge(s_qtp, u + 1)
                    nc.vector.tensor_tensor(dst[:, :, t * P:(t + 1) * P],
                                            ps[:, 7, 0:n * P].rearrange("p (k c) -> p k c", k=n),
                                            bcast(gain[:], 2, P), ALU.mult).then_inc(s_qt, 1)

                store_x(0)
                for t in range(NT):
                    if t + 1 < NT:
                        store_x(t + 1)
                    if t:
                        store_latent(t - 1)
                for u in range(NT - 1, 2 * NT):
                    store_latent(u)
                dve.wait_ge(s_lat, NT)
                a2 = gt[:, 0, :]
                st.done(nc.vector.tensor_tensor(a2.rearrange("p (x t) -> p x t", t=NT), abr[:, 0], bcast(dtb[:], 2, NT), ALU.add))
                st.settle()
                nc.vector.scalar_tensor_tensor(gt[:, 1, :], a2, -1.0, a2, ALU.mult, ALU.max).then_inc(s_gv, 1)
                st.done(nc.vector.tensor_scalar(gt[:, 2, :], a2, 0.0, None, ALU.max))
                dve.wait_ge(s_ga, 4)
                st.settle()
                st.done(nc.vector.tensor_tensor(gt[:, 2, :], gt[:, 2, :], gt[:, 1, :], ALU.add))
                st.done(nc.vector.tensor_scalar(gt[:, 3, :], gt[:, 3, :], 1.0, None, ALU.add))
                st.settle()
                nc.vector.scalar_tensor_tensor(gt[:, 4, :].rearrange("p (x t) -> p x t", t=NT),
                                               gt[:, 2, :].rearrange("p (x t) -> p x t", t=NT), -1.0,
                                               bcast(alog[:], 2, NT), ALU.mult, ALU.mult).then_inc(s_gv, 1)
                nc.vector.reciprocal(b_col[:], gt[:, 3, :]).then_inc(s_gv, 1)
                dve.wait_ge(s_gp, 1)
                nc.vector.tensor_copy(g_col[:], ps[:, 7, 0:96]).then_inc(s_gv, 1)
                dve.wait_ge(s_gp, 2)
                nc.vector.tensor_copy(rowsb[:, 0, :], ps[0:96, 6, 0:P]).then_inc(s_gv, 1)
                nc.vector.tensor_copy(rowsb[:, 1, :], ps[0:96, 6, P:2 * P]).then_inc(s_gv, 1)
                dve.wait_ge(s_cv, 1)
                nc.vector.tensor_copy(convT[:], ps[:, 5, 0:120]).then_inc(s_cv, 1)
                for v in range(2 * NT):
                    t, half = v % NT, v // NT
                    o = zs[:, t, 512 * half:512 * half + 512].rearrange("p (h c) -> p h c", c=P)
                    dve.wait_ge(s_ez, v + 1)
                    nc.vector.tensor_tensor(o, o, bcast(gng[:], 1, 4), ALU.mult).then_inc(s_z, 1)

            @block.tensor
            def _(pe):
                pe.wait_ge(s_const, 16 * 2)

                def transpose_x(t):
                    pe.wait_ge(s_xs, t + 1)
                    v = xs[t % 2][:, :].rearrange("p (c k) -> p k c", k=KD)
                    for b in range(4):
                        if t:
                            pe.wait_ge(s_xt, 4 * (t - 1) + b + 1)
                        for j in range(4):
                            last = nc.tensor.transpose(ps[:, 3 + b, j * P:(j + 1) * P], v[:, 4 * b + j, :], k.ident)
                        last.then_inc(s_xtp, 1)

                def project(u):
                    g, t = u // NT, u % NT
                    n = GROUPS[g][1] + (32 if g == 1 else 0)
                    if t == 0:
                        pe.wait_ge(s_w[g % 2], 16 * ((g // 2) + 1) + (16 if g % 2 else 0))
                    pe.wait_ge(s_xt, 4 * (t + 1))
                    if 3 <= u < NT + 3:
                        pe.wait_ge(s_qs, u - 2)
                    elif NT + 3 <= u < 2 * NT + 3:
                        pe.wait_ge(s_lat, u - NT - 2)
                    elif u >= 2 * NT + 3:
                        pe.wait_ge(s_ez, u - 2 * NT - 2)
                    for d in range(KD):
                        last = nc.tensor.matmul(ps[:, u % 3, 0:n], xT[:, d, t * P:(t + 1) * P], wb[g % 2][:, d, 0:n],
                                                start=(d == 0), stop=(d == KD - 1))
                    last.then_inc(s_acc, 1)

                def transpose_latent(u):
                    n = 4 if u < NT else 2
                    pe.wait_ge(s_qs, u + 1)
                    if u:
                        pe.wait_ge(s_qt, u)
                    v = ql[:, u % 2, 0:n * P].rearrange("p (c k) -> p k c", k=n)
                    for j in range(n):
                        last = nc.tensor.transpose(ps[:, 7, j * P:(j + 1) * P], v[:, j, :], k.ident)
                    last.then_inc(s_qtp, 1)

                transpose_x(0)
                for t in range(NT):
                    if t + 1 < NT:
                        transpose_x(t + 1)
                    project(t)
                    if t:
                        transpose_latent(t - 1)
                for u in range(NT, 2 * NT):
                    project(u)
                    transpose_latent(u - 1)
                project(2 * NT)
                transpose_latent(2 * NT - 1)
                project(2 * NT + 1)
                project(2 * NT + 2)
                pe.wait_ge(s_gv, 3)
                pe.wait_ge(s_qt, 2 * NT)
                for d in range(2):
                    last = nc.tensor.matmul(ps[:, 7, 48 * d:48 * d + 48], k.cum[d], gt[:, 4, 48 * d:48 * d + 48],
                                            start=True, stop=True)
                last.then_inc(s_gp, 1)
                pe.wait_ge(s_gv, 4)
                pe.wait_ge(s_xt, 4 * NT)
                nc.tensor.transpose(ps[0:96, 6, 0:P], g_col[:], k.ident)
                nc.tensor.transpose(ps[0:96, 6, P:2 * P], b_col[:], k.ident).then_inc(s_gp, 1)
                pe.wait_ge(s_const, NCONST)
                nc.tensor.transpose(ps[:, 5, 0:120], convr[:], k.ident[0:120, 0:120]).then_inc(s_cv, 1)
                for u in range(2 * NT + 3, 4 * NT):
                    project(u)


def attention(k):
    nc, a, ps = k.nc, k.a, k.psum
    units = [(h, s, t) for h in range(2) for s in range(2) for t in range(*SEGS[s])]
    NU = len(units)
    NB = 16
    with ExitStack() as c:
        sb = lambda n, s: k.sb(n, s, ctx=c)
        sem = lambda n: k.sem(n, c)
        wq = sb("wq", [P, 4, 2 * QH])
        wkv = sb("wkv", [P, 2, 2 * (NOPE + VH)])
        qraw = sb("qraw", [P, NT, 2, QH])
        kvraw = sb("kvraw", [P, NT, 2, NOPE + VH])
        qrot = sb("qrot", [P, NT, 2, ROPE])
        krot = sb("krot", [P, NT, 2, ROPE])
        kg = sb("kg", [P, NT, ROPE])
        kss = sb("kss", [P, NT])
        tmp = sb("tmp", [P, 4, NT, 2, HALF])
        ktmp = sb("ktmp", [P, 4, NT, HALF])
        gain = sb("gain", [P, 2, QH])
        gcol = sb("gcol", [P, 2])
        qT = sb("qT", [P, 2, T])
        kT = sb("kT", [P, 2, T])
        qrT = sb("qrT", [ROPE, 2, T])
        krT = sb("krT", [ROPE, 2, T])
        sq = sb("sq", [P, QH])
        ss = sb("ssq", [P, 4, NT])
        rs = sb("rsq", [P, 4, NT])
        mx = sb("mx", [P, NU])
        negb = sb("negb", [P, NU])
        rsum = sb("rsum", [P, NU])
        rinv = sb("rinv", [P, NU])
        pr = sb("pr", [P, 3, SS_])
        pT = sb("pT", [P, 2, 4, SS_])
        mix_sb = sb("mix_sb", [P, 2, T])
        eps_sb = sb("eps_b", [P, 1])

        s_w = sem("mla_weights")
        s_c = sem("mla_constants")
        s_proj = sem("mla_projected")
        s_raw = sem("mla_copied")
        s_sq = sem("mla_squared")
        s_kr = sem("k_rotated_once")
        s_rs = sem("mla_rms")
        s_kn = sem("k_normed")
        s_qr = sem("q_rotated")
        s_tp = sem("mla_transposed")
        s_ta = sem("mla_stored_scalar")
        s_tv = sem("mla_stored_vector")
        s_sc = sem("scores")
        s_mx = sem("score_max")
        s_ex = sem("probs_raw")
        s_p = sem("probs")
        s_pt = sem("probs_transposed")
        s_ptc = sem("probs_stored")
        s_o = sem("attended")
        s_mix = sem("mla_mixed")
        s_out = sem("mla_output")
        s_act = sem("mla_scalar_step")
        s_vec = sem("mla_vector_step")
        s_pool = sem("mla_pool_step")

        wq_d = a["w_q_b"][0].rearrange("(p k) n -> p k n", k=4)
        wkv_d = a["w_kv_b"][0].rearrange("(p k) n -> p k n", k=2)
        BATCHES = ([("q", h, b) for h in range(2) for b in range(2)] + [("k", h, b) for h in range(2) for b in range(2)]
                   + [("kr", h, b) for h in range(2) for b in range(2)] + [("qr", h, b) for h in range(2) for b in range(2)])
        cos2, sin2 = bcast(k.rope[:, :, 0, :], 2, 2), bcast(k.rope[:, :, 1, :], 2, 2)

        with nc.Block() as block:
            @block.sync
            def _(sp):
                sp.dma_start(gain[:, 0, :], a["q_norm_g"][0].partition_broadcast(P)).then_inc(s_c, 16)
                sp.dma_start(gain[:, 1, :], a["k_norm_g"][0].partition_broadcast(P)).then_inc(s_c, 16)
                sp.dma_start(gcol[:, 0:1], a["q_norm_g"][0, 0:NOPE].rearrange("(p o) -> p o", o=1)).then_inc(s_c, 16)
                sp.dma_start(gcol[:, 1:2], a["k_norm_g"][0, 0:NOPE].rearrange("(p o) -> p o", o=1)).then_inc(s_c, 16)
                sp.dma_start(wq[:], wq_d[:, :, 0:2 * QH]).then_inc(s_w, 16)
                sp.dma_start(wkv[:], wkv_d[:, :, 0:2 * (NOPE + VH)]).then_inc(s_w, 16)
                with sp.Fori(1, HP) as i:
                    wait_apart(sp, s_proj, i * (2 * NT), k)
                    wait_apart(sp, s_w, i * 32, k)
                    sp.dma_start(wq[:], wq_d[:, :, bass.ds(i * (2 * QH), 2 * QH)]).then_inc(s_w, 16)
                    sp.dma_start(wkv[:], wkv_d[:, :, bass.ds(i * (2 * (NOPE + VH)), 2 * (NOPE + VH))]).then_inc(s_w, 16)
                    wait_apart(sp, s_mix, i * 4 + 4, k)
                    sp.dma_start(k.mix[bass.ds(i * 2 - 2, 2)].rearrange("h p t -> p h t"), mix_sb[:]).then_inc(s_out, 16)
                sp.wait_ge(s_mix, HP * 4 + 4)
                sp.dma_start(k.mix[H - 2:H].rearrange("h p t -> p h t"), mix_sb[:]).then_inc(s_out, 16)
                sp.wait_ge(s_out, HP * 16 + 16)

            @block.tensor
            def _(pe):
                def transposes(i, b):
                    kind, h, half = BATCHES[b]
                    if b == 0:
                        pe.wait_ge(s_mix, i * 4 + 4)
                    elif 4 <= b < 8:
                        pe.wait_ge(s_ta, i * 8 + (b - 3))
                    elif b >= 8:
                        wait_apart(pe, s_tv, i * 8 + (b - 7), k)
                    if kind == "q":
                        pe.wait_ge(s_raw, i * (2 * NT) + 2 * (3 * half + 3))
                    elif b == 4:
                        pe.wait_ge(s_kn, i + 1)
                    elif b == 12:
                        wait_apart(pe, s_qr, i + 1, k)
                    for j in range(3):
                        t = 3 * half + j
                        src = {"q": qraw[:, t, h, 0:NOPE], "k": kvraw[:, t, h, 0:NOPE],
                               "qr": qrot[:, t, h, :], "kr": krot[:, t, h, :]}[kind]
                        n = NOPE if kind in "qk" else ROPE
                        last = nc.tensor.transpose(ps[0:n, 4 + b % 4, j * P:(j + 1) * P], src, k.ident)
                    last.then_inc(s_tp, 1)

                def scores(i, u):
                    h, s, t = units[u]
                    c0, S = SEGS[s][0] * P, (SEGS[s][1] - SEGS[s][0]) * P
                    bank = (0, 1, 6)[u % 3]
                    if u >= 3:
                        pe.wait_ge(s_ex, i * NU + (u - 2))
                    nc.tensor.matmul(ps[:, bank, 0:S], qT[:, h, t * P:(t + 1) * P], kT[:, h, c0:c0 + S], start=True, stop=False)
                    nc.tensor.matmul(ps[:, bank, 0:S], qrT[:, h, t * P:(t + 1) * P], krT[:, h, c0:c0 + S],
                                     start=False, stop=True).then_inc(s_sc, 1)

                def probs_t(i, u):
                    h, s, t = units[u]
                    n = SEGS[s][1] - SEGS[s][0]
                    pe.wait_ge(s_p, i * NU + u + 1)
                    if u >= 2:
                        pe.wait_ge(s_ptc, i * NU + u - 1)
                    for j in range(n):
                        last = nc.tensor.transpose(ps[:, 2 + u % 2, j * P:(j + 1) * P], pr[:, u % 3, j * P:(j + 1) * P], k.ident)
                    last.then_inc(s_pt, 1)

                def values(i, g):
                    h, s = g // 2, g % 2
                    t0, t1 = SEGS[s]
                    S = (t1 - t0) * P
                    last_u = max(u for u in range(NU) if units[u][:2] == (h, s))
                    pe.wait_ge(s_ptc, i * NU + last_u + 1)
                    if g >= 2:
                        pe.wait_ge(s_mix, i * 4 + 4 + g - 1)
                    for j in range(t1 - t0):
                        last = nc.tensor.matmul(ps[:, 4 + g % 2, 0:S], kvraw[:, t0 + j, h, NOPE:], pT[:, g % 2, j, 0:S],
                                                start=(j == 0), stop=(j == t1 - t0 - 1))
                    last.then_inc(s_o, 1)

                with pe.Fori(0, HP) as i:
                    pe.wait_ge(s_w, i * 32 + 32)
                    for t in range(NT):
                        b = t % 2
                        if t >= 2:
                            pe.wait_ge(s_raw, i * (2 * NT) + 2 * (t - 1))
                        for kk in range(4):
                            last = nc.tensor.matmul(ps[:, b, 0:2 * QH], k.qlT[:, kk, t * P:(t + 1) * P], wq[:, kk, :],
                                                    start=(kk == 0), stop=(kk == 3))
                        last.then_inc(s_proj, 1)
                        for kk in range(2):
                            last = nc.tensor.matmul(ps[:, 2 + b, :], k.kvlT[:, kk, t * P:(t + 1) * P], wkv[:, kk, :],
                                                    start=(kk == 0), stop=(kk == 1))
                        last.then_inc(s_proj, 1)
                    for b in range(NB):
                        transposes(i, b)
                    pe.wait_ge(s_ta, i * 8 + 8)
                    pe.wait_ge(s_tv, i * 8 + 8)
                    scores(i, 0)
                    scores(i, 1)
                    for u in range(NU):
                        if u + 2 < NU:
                            scores(i, u + 2)
                        probs_t(i, u)
                        if u + 1 < NU and units[u][:2] != units[u + 1][:2]:
                            pass
                        if u >= 1 and units[u - 1][:2] != units[u][:2]:
                            values(i, 2 * units[u - 1][0] + units[u - 1][1])
                    values(i, 3)

            @block.vector
            def _(dve):
                dve.sem_inc(s_mix, 4)
                dve.sem_inc(s_out, 16)
                nc.vector.memset(eps_sb[:], EPS).then_inc(s_kr, 1)
                dve.wait_ge(s_c, 64)
                st = Steps(dve, s_vec)
                st.done(nc.vector.tensor_tensor(kg[:], k.krope[:], k.krope[:], ALU.mult))
                st.settle()
                st.done(nc.vector.tensor_reduce(kss[:], kg[:], AX, ALU.add))
                st.settle()
                kr = k.krope[:]
                st.done(nc.vector.tensor_tensor(kr, kr, bcast(gain[:, 1, NOPE:], 1, NT), ALU.mult))
                st.settle()
                c1, s1 = k.rope[:, :, 0, :], k.rope[:, :, 1, :]
                for j, (x, y) in enumerate(((kr[:, :, 0:HALF], c1), (kr[:, :, HALF:], s1), (kr[:, :, HALF:], c1), (kr[:, :, 0:HALF], s1))):
                    st.done(nc.vector.tensor_tensor(ktmp[:, j], x, y, ALU.mult))
                st.settle()
                st.done(nc.vector.tensor_tensor(kg[:, :, 0:HALF], ktmp[:, 0], ktmp[:, 1], ALU.subtract))
                st.done(nc.vector.tensor_tensor(kg[:, :, HALF:], ktmp[:, 2], ktmp[:, 3], ALU.add))
                st.settle()
                base, per = st.n, 3 + 2 * NU

                with dve.Fori(0, HP) as i:
                    st = Steps(dve, s_vec, i * per + base)
                    for t in range(NT):
                        dve.wait_ge(s_proj, i * (2 * NT) + 2 * t + 1)
                        nc.vector.tensor_copy(qraw[:, t].rearrange("p h c -> p (h c)"), ps[:, t % 2, 0:2 * QH]).then_inc(s_raw, 1)
                        dve.wait_ge(s_proj, i * (2 * NT) + 2 * t + 2)
                        nc.vector.tensor_copy(kvraw[:, t].rearrange("p h c -> p (h c)"), ps[:, 2 + t % 2, :]).then_inc(s_raw, 1)
                    dve.wait_ge(s_sq, i * NT + NT)
                    st.done(nc.vector.tensor_tensor(ss[:, 2:4, :], ss[:, 2:4, :], bcast(kss[:], 1, 2), ALU.add))
                    dve.wait_ge(s_rs, i + 1)
                    dve.wait_ge(s_raw, i * (2 * NT) + 2 * NT)
                    kn = kvraw[:, :, :, 0:NOPE]
                    rk = rs[:, 2:4, :].rearrange("p h t -> p t h")
                    st.done(nc.vector.tensor_tensor(kn, kn, bcast(rk, 3, NOPE), ALU.mult))
                    nc.vector.tensor_tensor(krot[:], bcast(kg[:], 2, 2), bcast(rk, 3, ROPE), ALU.mult).then_inc(s_kn, 1)
                    st.done(nc.vector.tensor_scalar(rs[:, 0:2, :], rs[:, 0:2, :], QH ** -0.5, None, ALU.mult))
                    for b in range(4, 12):
                        kind, h, half = BATCHES[b]
                        dve.wait_ge(s_tp, i * NB + b + 1)
                        cols = slice(3 * half * P, 3 * half * P + 3 * P)
                        if kind == "k":
                            nc.vector.tensor_scalar(kT[:, h, cols], ps[:, 4 + b % 4, 0:3 * P], gcol[:, 1:2], None, ALU.mult).then_inc(s_tv, 1)
                        else:
                            nc.vector.tensor_copy(krT[:, h, cols], ps[0:ROPE, 4 + b % 4, 0:3 * P]).then_inc(s_tv, 1)

                    def maximum(u):
                        h, s, t = units[u]
                        S = (SEGS[s][1] - SEGS[s][0]) * P
                        dve.wait_ge(s_sc, i * NU + u + 1)
                        st.done(nc.vector.reduce_max(mx[:, u:u + 1], ps[:, (0, 1, 6)[u % 3], 0:S], AX))
                        st.settle()
                        nc.vector.scalar_tensor_tensor(negb[:, u:u + 1], mx[:, u:u + 1], -1.0, rs[:, h, t:t + 1],
                                                       ALU.mult, ALU.mult).then_inc(s_mx, 1)

                    def scale(u):
                        h, s, t = units[u]
                        S = (SEGS[s][1] - SEGS[s][0]) * P
                        dve.wait_ge(s_ex, i * NU + u + 1)
                        st.done(nc.vector.reciprocal(rinv[:, u:u + 1], rsum[:, u:u + 1]))
                        st.settle()
                        nc.vector.tensor_scalar(pr[:, u % 3, 0:S], pr[:, u % 3, 0:S], rinv[:, u:u + 1], None, ALU.mult).then_inc(s_p, 1)

                    def mix(g):
                        h, s = g // 2, g % 2
                        c0, S = SEGS[s][0] * P, (SEGS[s][1] - SEGS[s][0]) * P
                        dve.wait_ge(s_o, i * 4 + g + 1)
                        if g == 0:
                            dve.wait_ge(s_out, i * 16 + 16)
                        nc.vector.tensor_copy(mix_sb[:, h, c0:c0 + S], ps[:, 4 + g % 2, 0:S]).then_inc(s_mix, 1)

                    for u in range(NU + 1):
                        if u < NU:
                            maximum(u)
                        if u >= 1:
                            scale(u - 1)
                        if u >= 4 and units[u - 3][:2] != units[u - 4][:2]:
                            mix(2 * units[u - 4][0] + units[u - 4][1])
                    mix(3)
                    assert st.n == per, st.n

            @block.gpsimd
            def _(pool):
                pool.wait_ge(s_c, 64)
                per = 5
                with pool.Fori(0, HP) as i:
                    st = Steps(pool, s_pool, i * per)
                    pool.wait_ge(s_sq, i * NT + NT)
                    qr = qraw[:, :, :, NOPE:]
                    st.done(nc.gpsimd.tensor_tensor(qr, qr, bcast(bcast(gain[:, 0, NOPE:], 1, 2), 1, NT), ALU.mult))
                    st.settle()
                    for j, (x, y) in enumerate(((qr[..., 0:HALF], cos2), (qr[..., HALF:], sin2), (qr[..., HALF:], cos2), (qr[..., 0:HALF], sin2))):
                        st.done(nc.gpsimd.tensor_tensor(tmp[:, j], x, y, ALU.mult))
                    st.settle()
                    pool.wait_ge(s_tp, i * NB + 1)
                    nc.gpsimd.tensor_tensor(qrot[..., 0:HALF], tmp[:, 0], tmp[:, 1], ALU.subtract)
                    nc.gpsimd.tensor_tensor(qrot[..., HALF:], tmp[:, 2], tmp[:, 3], ALU.add).then_inc(s_qr, 1)
                    assert st.n == per, st.n

            @block.scalar
            def _(act):
                act.preload_act_table_set(TABLES)
                act.wait_ge(s_kr, 1)
                act.wait_ge(s_c, 64)
                per = 3 * NT + 1
                with act.Fori(0, HP) as i:
                    st = Steps(act, s_act, i * per)
                    for t in range(NT):
                        act.wait_ge(s_raw, i * (2 * NT) + 2 * t + 2)
                        for j in range(4):
                            x = qraw[:, t, j, :] if j < 2 else kvraw[:, t, j - 2, 0:NOPE]
                            st.settle()
                            ins = nc.scalar.activation(sq[:, 0:QH if j < 2 else NOPE], x, ACT.Square, accum_out=ss[:, j, t:t + 1])
                            if j < 3:
                                st.done(ins)
                            else:
                                ins.then_inc(s_sq, 1)
                                act.wait_ge(s_sq, i * NT + t + 1)
                    act.wait_ge(s_vec, i * (3 + 2 * NU) + 10)
                    st.done(nc.scalar.activation(ss[:], ss[:], ACT.Ln, bias=eps_sb[:], scale=1.0 / QH))
                    st.settle()
                    nc.scalar.activation(rs[:], ss[:], ACT.Exp, scale=-0.5).then_inc(s_rs, 1)
                    for b in (0, 1, 2, 3, 12, 13, 14, 15):
                        kind, h, half = BATCHES[b]
                        act.wait_ge(s_tp, i * NB + b + 1)
                        cols = slice(3 * half * P, 3 * half * P + 3 * P)
                        if kind == "q":
                            nc.scalar.activation(qT[:, h, cols], ps[:, 4 + b % 4, 0:3 * P], ACT.Copy, scale=gcol[:, 0:1]).then_inc(s_ta, 1)
                        else:
                            nc.scalar.copy(qrT[:, h, cols], ps[0:ROPE, 4 + b % 4, 0:3 * P]).then_inc(s_ta, 1)

                    def exponent(u):
                        h, s, t = units[u]
                        S = (SEGS[s][1] - SEGS[s][0]) * P
                        act.wait_ge(s_mx, i * NU + u + 1)
                        if u >= 3:
                            act.wait_ge(s_pt, i * NU + u - 2)
                        nc.scalar.activation(pr[:, u % 3, 0:S], ps[:, (0, 1, 6)[u % 3], 0:S], ACT.Exp, bias=negb[:, u:u + 1],
                                             scale=rs[:, h, t:t + 1], accum_out=rsum[:, u:u + 1]).then_inc(s_ex, 1)

                    def store_probs(u):
                        h, s, t = units[u]
                        n = SEGS[s][1] - SEGS[s][0]
                        g = 2 * h + s
                        q0 = (t - SEGS[s][0]) * P
                        act.wait_ge(s_pt, i * NU + u + 1)
                        if g >= 2 and (u == 0 or units[u - 1][:2] != units[u][:2]):
                            act.wait_ge(s_o, i * 4 + g - 1)
                        nc.scalar.copy(pT[:, g % 2, 0:n, q0:q0 + P], ps[:, 2 + u % 2, 0:n * P].rearrange("p (j q) -> p j q", q=P)).then_inc(s_ptc, 1)

                    for u in range(NU + 1):
                        if u < NU:
                            exponent(u)
                        if u >= 1:
                            store_probs(u - 1)
                    assert st.n == per, st.n
    k.mla_ctx.close()


GROUPS = [(s, n) for n in range(2) for s in range(2)] + [(1, 2), (1, 3)]
NG = len(GROUPS)


def group_tiles(g):
    s, n = GROUPS[g]
    return SEGS[s][0] + n, SEGS[s][1] - 1 - n


def is_last(g):
    s, n = GROUPS[g]
    return n == SEGS[s][1] - SEGS[s][0] - 1


def deltanet(k):
    nc, a, ps = k.nc, k.a, k.psum
    TYPES = (1, 2, 0)
    NC = 6
    LV = LEVELS - 1
    PAD = 2 + SP_ + 4 + SS_ + 2
    with ExitStack() as c:
        sb = lambda n, s: k.sb(n, s, ctx=c)
        sem = lambda n: k.sem(n, c)
        blocks = sb("blocks", [P, LEVELS, 3, P])
        wg = sb("wg", [P, 2, KD, 2 * P])
        kq = sb("kq", [P, 2, 2, T])
        ktok = sb("ktok", [P, NT, 2, P])
        vtok = sb("vtok", [P, NT, 2, P])
        obuf = sb("obuf", [P, 2, NT, 2, P])
        vch = obuf[:, 0].rearrange("p t h c -> p (t h c)").rearrange("p (h t) -> p h t", h=2)
        pre = sb("pre", [P, 2, PAD])
        work = sb("work", [P, 16 * P])
        y = work[:, 0:2 * PAD].rearrange("p (b c) -> p b c", b=2)
        p1 = work[:, 0:8 * P].rearrange("p (x n c) -> p x n c", x=2, n=4)
        rv = work[:, 8 * P:12 * P].rearrange("p (n c) -> p n c", n=4)
        vn = work[:, 12 * P:16 * P].rearrange("p (n c) -> p n c", n=4)
        mix_sb = sb("mix_g", [P, 2, T])
        lt = mix_sb[:].rearrange("p h t -> p (h t)")[:, 0:8 * P].rearrange("p (x n c) -> p x n c", x=2, n=4)
        inv = sb("inv", [P, 16 * P])
        tinv = inv[:, 0:8 * P].rearrange("p (x n c) -> p x n c", x=2, n=4)
        tt = inv[:, 8 * P:16 * P].rearrange("p (x n c) -> p x n c", x=2, n=4)
        zg = inv[:, 0:2 * NT * P].rearrange("p (t c) -> p t c", t=NT)
        ones = sb("ones", [P, P])
        rows = sb("rows", [P, 2, 4, 2, P])
        dt = sb("dt", [P, 2, 4, P])
        intra = sb("intra", [P, 2, 2, 4, P])
        kd = sb("kd", [P, 2, 2, 4, P])
        qd = sb("qd", [P, 2, 2, 4, P])
        tf = sb("tf", [P, 2, 2, 4, P])
        state = sb("state", [P, 2, 4, P])
        ctap = sb("ctap", [P, 5, 3, 2])
        gcp = sb("gcp", [P, 4, NT])
        ngc = sb("ngc", [P, 4, NT])
        neg = sb("neg", [P, 4, NT])
        bcp = sb("bcp", [P, 4, NT])
        edl = sb("edl", [P, 2, 4])
        egl = sb("egl", [P, 2, 2, 4])
        oss = sb("oss", [P, NT * 2])
        ors = sb("ors", [P, NT * 2])
        eps_sb = sb("eps_c", [P, 1])

        s_m = sem("block_masks_loaded")
        s_init = sem("deltanet_constants")
        s_w = [sem("kq_weights"), sem("v_weights")]
        s_z = sem("z_loaded")
        s_rows = [sem("rows_loaded0"), sem("rows_loaded1")]
        s_col = sem("columns_ready")
        s_proj = sem("qkv_projected")
        s_pre = sem("qkv_copied")
        s_conv = sem("convolved")
        s_silu = sem("silu_done")
        s_sq = sem("kq_squared")
        s_ssum = sem("kq_summed")
        s_rn = sem("kq_rms")
        s_nrm = sem("kq_normed")
        s_kvt = sem("kv_transposed")
        s_kvc = sem("kv_stored")
        s_gram = sem("gram")
        s_dtin = sem("decay_masked")
        s_dt = sem("decay_matrix")
        s_eg = sem("decay_vectors")
        s_lt = sem("lower_matrix")
        s_qd = sem("decayed_kq")
        s_tt = [sem("inverse_t0"), sem("inverse_t1")]
        s_tr = [sem("inverse_transposed0"), sem("inverse_transposed1")]
        s_t = [sem("inverse0"), sem("inverse1")]
        s_m1 = [sem("level_product0"), sem("level_product1")]
        s_p1 = [sem("level_masked0"), sem("level_masked1")]
        s_m2 = [sem("level_update0"), sem("level_update1")]
        s_tf = sem("inverse_beta")
        s_ks = sem("state_read")
        s_r = sem("residual_values")
        s_vn = sem("new_values")
        s_vc = sem("new_values_stored")
        s_o = sem("chunk_output")
        s_oc = sem("chunk_output_stored")
        s_sn = sem("state_product")
        s_st = sem("state_updated")
        s_oss = sem("output_squares")
        s_ors = sem("output_rms")
        s_on = sem("output_gated")
        s_ot = sem("output_transposed")
        s_om = sem("output_stored")
        s_out = sem("deltanet_output")
        s_act = sem("deltanet_scalar_step")
        s_vec = sem("deltanet_vector_step")
        s_pool = sem("deltanet_pool_step")

        w_d = a["w_in"][0].rearrange("(p k) n -> p k n", k=KD)
        scan_steps = lambda g: GROUPS[g][1] > 0
        n_ks = sum(scan_steps(g) for g in range(NG))
        n_sn = sum(not is_last(g) for g in range(NG))
        ks_at = lambda g: sum(scan_steps(x) for x in range(g + 1))
        sn_at = lambda g: sum(not is_last(x) for x in range(g + 1))

        with nc.Block() as block:
            @block.sync
            def _(sp):
                def load_w(i, j):
                    c0 = C_QKV + TYPES[j] * GW
                    sp.dma_start(wg[:, j % 2], w_d[:, :, bass.ds(i * (2 * P) + c0, 2 * P)]).then_inc(s_w[j % 2], 16)

                def load_rows(i, g):
                    wait_apart(sp, s_lt, i * NG + g + 1, k)
                    wait_apart(sp, s_qd, i * NG + g + 1, k)
                    tiles = group_tiles(g)
                    for d in range(2):
                        src = k.rows[d, tiles[d], bass.ds(i * 2, 2)]
                        sp.dma_start(rows[:, g % 2, 2 * d:2 * d + 2], src.partition_broadcast(P)).then_inc(s_rows[g % 2], 16)

                def pair(i, more):
                    wait_apart(sp, s_proj, i * NC + 2, k)
                    wait_apart(sp, s_w[0], i * 32 + 16, k)
                    load_w(i, 2)
                    load_rows(i, 0)
                    load_rows(i, 1)
                    for g in range(2, NG):
                        load_rows(i, g)
                    wait_apart(sp, s_tf, i * NG + NG, k)
                    sp.dma_start(zg[:], k.zs[:, :, bass.ds(i * (2 * P), 2 * P)].rearrange("t p c -> p t c")).then_inc(s_z, 16)
                    if more:
                        wait_apart(sp, s_proj, i * NC + NC, k)
                        wait_apart(sp, s_w[0], i * 32 + 32, k)
                        wait_apart(sp, s_w[1], i * 16 + 16, k)
                        load_w(i + 1, 0)
                        load_w(i + 1, 1)
                    wait_apart(sp, s_om, i * 4 + 8, k)
                    sp.dma_start(k.mix[bass.ds(i * 2 + H, 2)].rearrange("h p t -> p h t"), mix_sb[:]).then_inc(s_out, 16)

                sp.dma_start(blocks[:].rearrange("p l d i -> p (l d i)"), a["square"][:, 5 * P:]).then_inc(s_m, 16)
                load_w(0, 0)
                load_w(0, 1)
                with sp.Fori(0, HP - 1) as i:
                    pair(i, True)
                pair(HP - 1, False)
                sp.wait_ge(s_out, HP * 16 + 16)

            @block.tensor
            def _(pe):
                def project(i, c):
                    j, h = c // 2, c % 2
                    if c == 0:
                        pe.wait_ge(s_om, i * 4 + 4)
                    elif c >= 2:
                        pe.wait_ge(s_pre, i * NC + c - 1)
                    if h == 0:
                        pe.wait_ge(s_w[j % 2], i * (32, 16)[j % 2] + (16 if j < 2 else 32))
                    b = 2 * (c % 2)
                    for d in range(KD):
                        w = wg[:, j % 2, d, h * P:(h + 1) * P]
                        nc.tensor.matmul(ps[:, b, 0:SS_], w, k.xT[:, d, SP_:T], start=(d == 0), stop=(d == KD - 1))
                        last = nc.tensor.matmul(ps[:, b + 1, 0:SP_], w, k.xT[:, d, 0:SP_], start=(d == 0), stop=(d == KD - 1))
                    last.then_inc(s_proj, 1)

                def sum_squares(i, n):
                    pe.wait_ge(s_sq, i * 4 + n + 1)
                    if n >= 2:
                        pe.wait_ge(s_rn, i * 4 + n - 1)
                    b = 4 + 2 * (n % 2)
                    nc.tensor.matmul(ps[:, b, 0:SS_], ones[:], y[:, n % 2, SP_:T], start=True, stop=True)
                    nc.tensor.matmul(ps[:, b + 1, 0:SP_], ones[:], y[:, n % 2, 0:SP_], start=True, stop=True).then_inc(s_ssum, 1)

                def transposes(i, b):
                    if b == 0:
                        pe.wait_ge(s_pre, i * NC + NC)
                        pe.wait_ge(s_silu, i * NC + 4)
                    elif b == 3:
                        pe.wait_ge(s_nrm, i * 4 + 2)
                    elif b > 3:
                        pe.wait_ge(s_kvc, i * 6 + b - 3)
                    for m in range(4):
                        t, h = 2 * (b % 3) + m // 2, m % 2
                        src = (vch[:, h] if b < 3 else kq[:, h, 0])[:, t * P:(t + 1) * P]
                        last = nc.tensor.transpose(ps[:, b % 4, m * P:(m + 1) * P], src, k.ident)
                    last.then_inc(s_kvt, 1)

                def gram(i, g):
                    x, r = g % 2, g // 2
                    if r == 0:
                        pe.wait_ge(s_kvc, i * 6 + 6)
                        pe.wait_ge(s_nrm, i * 4 + 4)
                    else:
                        pe.wait_ge(s_tt[x], i * 21 + 7 * r)
                    tiles = group_tiles(g)
                    for d in range(2):
                        cols = slice(tiles[d] * P, tiles[d] * P + P)
                        for h in range(2):
                            last = nc.tensor.matmul(ps[:, 2 * x + d, 2 * h * P:2 * (h + 1) * P], kq[:, h, 0, cols],
                                                    kq[:, h, :, cols], start=True, stop=True)
                    last.then_inc(s_gram, 1)

                def back(i, r, x, lv):
                    pe.wait_ge(s_tt[x], i * 21 + 7 * r + lv + 1)
                    for n in range(4):
                        last = nc.tensor.transpose(ps[:, 2 * x, n * P:(n + 1) * P], tt[:, x, n], k.ident)
                    last.then_inc(s_tr[x], 1)

                def product(i, r, x, lv):
                    pe.wait_ge(s_t[x], i * 18 + 6 * r + lv)
                    for n in range(4):
                        last = nc.tensor.matmul(ps[:, 2 * x, n * P:(n + 1) * P], lt[:, x, n], tinv[:, x, n], start=True, stop=True)
                    last.then_inc(s_m1[x], 1)

                def update(i, r, x, lv):
                    pe.wait_ge(s_p1[x], i * 18 + 6 * r + lv)
                    for n in range(4):
                        last = nc.tensor.matmul(ps[:, 2 * x + 1, n * P:(n + 1) * P], p1[:, x, n], tt[:, x, n], start=True, stop=True)
                    last.then_inc(s_m2[x], 1)

                def scan(i, g, part):
                    x, par, s = g % 2, (g // 2) % 2, GROUPS[g][0]
                    z, tiles = 4 + 2 * x, group_tiles(g)
                    if part == 0 and scan_steps(g):
                        pe.wait_ge(s_st, i * n_sn + sn_at(g - 1 if GROUPS[g - 1][0] == s else g - 2))
                        if g >= 2:
                            pe.wait_ge(s_oc, i * NG + g - 1)
                        for n in range(4):
                            t = tiles[n // 2]
                            last = nc.tensor.matmul(ps[:, z, n * P:(n + 1) * P], kq[:, n % 2, 0, t * P:(t + 1) * P],
                                                    state[:, s, n], start=True, stop=True)
                        last.then_inc(s_ks, 1)
                    if part == 1:
                        pe.wait_ge(s_tf, i * NG + g + 1)
                        if scan_steps(g):
                            pe.wait_ge(s_r, i * n_ks + ks_at(g))
                        for n in range(4):
                            rhs = rv[:, n] if scan_steps(g) else vtok[:, tiles[n // 2], n % 2, :]
                            last = nc.tensor.matmul(ps[:, z + 1, n * P:(n + 1) * P], tf[:, par, x, n], rhs, start=True, stop=True)
                        last.then_inc(s_vn, 1)
                    if part == 2:
                        pe.wait_ge(s_vc, i * NG + g + 1)
                        pe.wait_ge(s_qd, i * NG + g + 3)
                        for n in range(4):
                            if scan_steps(g):
                                nc.tensor.matmul(ps[:, z, n * P:(n + 1) * P], qd[:, par, x, n], state[:, s, n], start=True, stop=False)
                            last = nc.tensor.matmul(ps[:, z, n * P:(n + 1) * P], intra[:, par, x, n], vn[:, n],
                                                    start=not scan_steps(g), stop=True)
                        last.then_inc(s_o, 1)
                        if not is_last(g):
                            for n in range(4):
                                last = nc.tensor.matmul(ps[:, z + 1, n * P:(n + 1) * P], kd[:, par, x, n], vn[:, n], start=True, stop=True)
                            last.then_inc(s_sn, 1)

                pe.wait_ge(s_init, 3)
                with pe.Fori(0, HP) as i:
                    for c in range(NC):
                        project(i, c)
                    for b in range(3):
                        transposes(i, b)
                    for n in range(4):
                        sum_squares(i, n)
                    for b in range(3, 6):
                        transposes(i, b)
                    for r in range(3):
                        for x in range(2):
                            gram(i, 2 * r + x)
                        for x in range(2):
                            back(i, r, x, 0)
                        for lv in range(1, LV + 1):
                            for x in range(2):
                                product(i, r, x, lv)
                            if r:
                                scan(i, 2 * (r - 1) + (lv - 1) // 3, (lv - 1) % 3)
                            for x in range(2):
                                update(i, r, x, lv)
                            if lv < LV:
                                for x in range(2):
                                    back(i, r, x, lv)
                    for g in (4, 5):
                        for part in range(3):
                            scan(i, g, part)
                    pe.wait_ge(s_on, i + 1)
                    for b in range(4):
                        h, half = b // 2, b % 2
                        for m in range(3):
                            t = 3 * half + m
                            last = nc.tensor.transpose(ps[:, b, m * P:(m + 1) * P], obuf[:, 0, t, h, :], k.ident)
                        last.then_inc(s_ot, 1)

            @block.scalar
            def _(act):
                act.sem_inc(s_om, 4)
                act.wait_ge(s_init, 3)
                per = 6 + NG

                def copy_tile(i, c):
                    act.wait_ge(s_proj, i * NC + c + 1)
                    if c >= 2:
                        act.wait_ge(s_conv, i * NC + c - 1)
                    b = 2 * (c % 2)
                    nc.scalar.copy(pre[:, c % 2, 2 + SP_ + 4:2 + SP_ + 4 + SS_], ps[:, b, 0:SS_])
                    nc.scalar.copy(pre[:, c % 2, 2:2 + SP_], ps[:, b + 1, 0:SP_]).then_inc(s_pre, 1)

                def silu(i, c):
                    h = c % 2
                    dst = kq[:, h, 0] if c < 2 else vch[:, h] if c < 4 else kq[:, h, 1]
                    act.wait_ge(s_conv, i * NC + c + 1)
                    nc.scalar.activation(dst[:, 0:SP_], y[:, c % 2, 0:SP_], ACT.Silu)
                    nc.scalar.activation(dst[:, SP_:T], y[:, c % 2, SP_ + 4:SP_ + 4 + SS_], ACT.Silu).then_inc(s_silu, 1)

                def square(i, n):
                    if n >= 2:
                        act.wait_ge(s_ssum, i * 4 + n - 1)
                    nc.scalar.activation(y[:, n % 2, 0:T], kq[:, n % 2, n // 2], ACT.Square).then_inc(s_sq, 1)

                def rms(i, n, st):
                    act.wait_ge(s_ssum, i * 4 + n + 1)
                    if n == 0:
                        act.wait_ge(s_out, i * 16 + 16)
                    if n >= 2:
                        act.wait_ge(s_nrm, i * 4 + n - 1)
                    b = 4 + 2 * (n % 2)
                    nc.scalar.activation(mix_sb[:, n % 2, SP_:T], ps[:, b, 0:SS_], ACT.Ln, bias=eps_sb[:])
                    st.done(nc.scalar.activation(mix_sb[:, n % 2, 0:SP_], ps[:, b + 1, 0:SP_], ACT.Ln, bias=eps_sb[:]))
                    st.settle()
                    nc.scalar.activation(mix_sb[:, n % 2, :], mix_sb[:, n % 2, :], ACT.Exp, scale=-0.5).then_inc(s_rn, 1)

                def store_kv(i, b):
                    act.wait_ge(s_kvt, i * 6 + b + 1)
                    dst = vtok if b < 3 else ktok
                    t = 2 * (b % 3)
                    nc.scalar.copy(dst[:, t:t + 2].rearrange("p t h c -> p (t h c)"), ps[:, b % 4, :]).then_inc(s_kvc, 1)

                def decay(i, g):
                    x, tiles = g % 2, group_tiles(g)
                    act.wait_ge(s_dtin, i * NG + g + 1)
                    for n in range(4):
                        t = tiles[n // 2]
                        last = nc.scalar.activation(dt[:, x, n], dt[:, x, n], ACT.Exp, bias=ngc[:, n, t:t + 1])
                    last.then_inc(s_dt, 1)

                def vectors(i, g, st):
                    x, par, tiles = g % 2, (g // 2) % 2, group_tiles(g)
                    act.wait_ge(s_rows[x], i * 96 + (g // 2 + 1) * 32)
                    for d in range(2):
                        end = P - 1 if d == 0 else 0
                        nc.scalar.activation(egl[:, par, x, 2 * d:2 * d + 2], rows[:, x, 2 * d:2 * d + 2, 0, end], ACT.Exp)
                        for h in range(2):
                            n = 2 * d + h
                            last = nc.scalar.activation(edl[:, x, n:n + 1], ngc[:, n, tiles[d]:tiles[d] + 1], ACT.Exp,
                                                        bias=rows[:, x, n, 0, end:end + 1])
                    st.done(last)
                    st.settle()
                    row = rows[:, x, :, 0]
                    nc.scalar.activation(row, row, ACT.Exp).then_inc(s_eg, 1)

                def store_inverse(i, r, x, lv):
                    act.wait_ge(s_tr[x], i * 18 + 6 * r + lv + 1)
                    nc.scalar.copy(tinv[:, x].rearrange("p n c -> p (n c)"), ps[:, 2 * x, :]).then_inc(s_t[x], 1)

                def scan(i, g, part):
                    x, tiles = g % 2, group_tiles(g)
                    z = 4 + 2 * x
                    if part == 1:
                        act.wait_ge(s_vn, i * NG + g + 1)
                        nc.scalar.copy(vn[:].rearrange("p n c -> p (n c)"), ps[:, z + 1, :]).then_inc(s_vc, 1)
                    if part == 2:
                        act.wait_ge(s_o, i * NG + g + 1)
                        for d in range(2):
                            last = nc.scalar.copy(obuf[:, d, tiles[d]].rearrange("p h c -> p (h c)"), ps[:, z, 2 * d * P:2 * (d + 1) * P])
                        last.then_inc(s_oc, 1)

                with act.Fori(0, HP) as i:
                    st = Steps(act, s_act, i * per)
                    act.preload_act_table_set("silu_and_others")
                    copy_tile(i, 0)
                    for c in range(NC):
                        silu(i, c)
                        if c + 1 < NC:
                            copy_tile(i, c + 1)
                    act.preload_act_table_set(TABLES)
                    act.wait_ge(s_silu, i * NC + NC)
                    act.wait_ge(s_col, i * 2 + 1)
                    st.done(nc.scalar.activation(neg[:], gcp[:], ACT.Exp))
                    square(i, 0)
                    square(i, 1)
                    for b in range(3):
                        store_kv(i, b)
                    rms(i, 0, st)
                    square(i, 2)
                    rms(i, 1, st)
                    square(i, 3)
                    rms(i, 2, st)
                    rms(i, 3, st)
                    for b in range(3, 6):
                        store_kv(i, b)
                    for g in (0, 1):
                        decay(i, g)
                        vectors(i, g, st)
                    for r in range(3):
                        for x in range(2):
                            store_inverse(i, r, x, 0)
                        for lv in range(1, LV + 1):
                            if r:
                                scan(i, 2 * (r - 1) + (lv - 1) // 3, (lv - 1) % 3)
                            if r < 2 and lv in (2, 3):
                                decay(i, 2 * (r + 1) + lv - 2)
                            if r < 2 and lv in (4, 5):
                                vectors(i, 2 * (r + 1) + lv - 4, st)
                            if lv < LV:
                                for x in range(2):
                                    store_inverse(i, r, x, lv)
                    for g in (4, 5):
                        scan(i, g, 1)
                        scan(i, g, 2)
                    act.wait_ge(s_oss, i + 1)
                    st.done(nc.scalar.activation(oss[:], oss[:], ACT.Ln, bias=eps_sb[:], scale=1.0 / P))
                    st.settle()
                    nc.scalar.activation(ors[:], oss[:], ACT.Exp, scale=-0.5).then_inc(s_ors, 1)
                    for b in range(4):
                        h, half = b // 2, b % 2
                        act.wait_ge(s_ot, i * 4 + b + 1)
                        nc.scalar.copy(mix_sb[:, h, 3 * half * P:3 * (half + 1) * P], ps[:, b, 0:3 * P]).then_inc(s_om, 1)
                    assert st.n == per, st.n

            @block.vector
            def _(dve):
                nc.vector.memset(eps_sb[:], EPS).then_inc(s_init, 1)
                nc.vector.memset(ones[:], 1.0).then_inc(s_init, 1)
                nc.vector.memset(pre[:], 0.0).then_inc(s_init, 1)
                dve.sem_inc(s_out, 16)
                dve.sem_inc(s_lt, 2)
                dve.wait_ge(s_m, 16)
                per = 1 + 4 * NC + 3 * NG + 3
                cv = k.convT[:].rearrange("p (w x h) -> p w x h", w=5, x=3)
                gv = k.g_col[:].rearrange("p (d h t) -> p d h t", d=2, h=H)
                bv = k.b_col[:].rearrange("p (d h t) -> p d h t", d=2, h=H)

                def convolve(i, c, st):
                    j, h = c // 2, c % 2
                    n = SP_ + 4 + SS_
                    o = y[:, c % 2, 0:n]
                    dve.wait_ge(s_pre, i * NC + c + 1)
                    if c >= 2:
                        dve.wait_ge(s_silu, i * NC + c - 1)
                    for w in range(5):
                        x, tap = pre[:, c % 2, w:w + n], ctap[:, w, TYPES[j], h:h + 1]
                        if w == 0:
                            st.done(nc.vector.tensor_scalar(o, x, tap, None, ALU.mult))
                        else:
                            st.settle()
                            ins = nc.vector.scalar_tensor_tensor(o, x, tap, o, ALU.mult, ALU.add)
                            ins.then_inc(s_conv, 1) if w == 4 else st.done(ins)

                def normalise(i, n):
                    dve.wait_ge(s_rn, i * 4 + n + 1)
                    v = kq[:, n % 2, n // 2]
                    nc.vector.scalar_tensor_tensor(v, v, P ** -0.5 if n >= 2 else 1.0, mix_sb[:, n % 2, :],
                                                   ALU.mult, ALU.mult).then_inc(s_nrm, 1)

                def lower(i, g, st):
                    x, par = g % 2, (g // 2) % 2
                    dve.wait_ge(s_gram, i * NG + g + 1)
                    dve.wait_ge(s_dt, i * NG + g + 1)
                    dve.wait_ge(s_rows[x], i * 96 + (g // 2 + 1) * 32)
                    for d in range(2):
                        m = ps[:, 2 * x + d, :].rearrange("p (h q c) -> p h q c", h=2, q=2)
                        nc.vector.tensor_tensor(intra[:, par, x, 2 * d:2 * d + 2], m[:, :, 1, :], dt[:, x, 2 * d:2 * d + 2], ALU.mult)
                        st.done(nc.vector.tensor_tensor(lt[:, x, 2 * d:2 * d + 2], m[:, :, 0, :], dt[:, x, 2 * d:2 * d + 2], ALU.mult))
                    st.settle()
                    nc.vector.tensor_tensor(lt[:, x], lt[:, x], rows[:, x, :, 1], ALU.mult).then_inc(s_lt, 1)
                    dve.wait_ge(s_lt, i * NG + g + 3)
                    four = lambda v: v.rearrange("p (d h) c -> p d h c", d=2)
                    st.done(nc.vector.tensor_tensor(four(p1[:, x]), four(lt[:, x]), bcast(blocks[:, 0, 0:2], 2, 2), ALU.mult))
                    st.settle()
                    if g >= 2:
                        dve.wait_ge(s_tf, i * NG + g - 1)
                    nc.vector.tensor_tensor(tt[:, x], bcast(k.ident, 1, 4), p1[:, x], ALU.subtract).then_inc(s_tt[x], 1)

                def mask(i, r, x, lv):
                    dve.wait_ge(s_m1[x], i * 18 + 6 * r + lv)
                    nc.vector.tensor_tensor(p1[:, x].rearrange("p (d h) c -> p d h c", d=2),
                                            ps[:, 2 * x, :].rearrange("p (d h c) -> p d h c", d=2, h=2),
                                            bcast(blocks[:, lv, 1:3], 2, 2), ALU.mult).then_inc(s_p1[x], 1)

                def advance(i, r, x, lv):
                    dve.wait_ge(s_m2[x], i * 18 + 6 * r + lv)
                    flat = tt[:, x].rearrange("p n c -> p (n c)")
                    nc.vector.tensor_tensor(flat, flat, ps[:, 2 * x + 1, :], ALU.subtract).then_inc(s_tt[x], 1)

                def scan(i, g, part):
                    x, par, s, tiles = g % 2, (g // 2) % 2, GROUPS[g][0], group_tiles(g)
                    z = 4 + 2 * x
                    if part == 0 and scan_steps(g):
                        dve.wait_ge(s_ks, i * n_ks + ks_at(g))
                        for n in range(4):
                            t = tiles[n // 2]
                            last = nc.vector.scalar_tensor_tensor(rv[:, n], ps[:, z, n * P:(n + 1) * P], neg[:, n, t:t + 1],
                                                                  vtok[:, t, n % 2, :], ALU.mult, ALU.add)
                        last.then_inc(s_r, 1)
                    if part == 2 and not is_last(g):
                        dve.wait_ge(s_sn, i * n_sn + sn_at(g))
                        for n in range(4):
                            o, p = state[:, s, n], ps[:, z + 1, n * P:(n + 1) * P]
                            if scan_steps(g):
                                last = nc.vector.scalar_tensor_tensor(o, o, egl[:, par, x, n:n + 1], p, ALU.mult, ALU.add)
                            else:
                                last = nc.vector.tensor_copy(o, p)
                        last.then_inc(s_st, 1)

                with dve.Fori(0, HP) as i:
                    st = Steps(dve, s_vec, i * per)
                    nc.vector.tensor_copy(ctap[:], cv[:, :, :, bass.ds(i * 2, 2)])
                    st.done(nc.vector.tensor_copy(gcp[:].rearrange("p (d h) t -> p d h t", d=2), gv[:, :, bass.ds(i * 2, 2), :]))
                    nc.vector.tensor_copy(bcp[:].rearrange("p (d h) t -> p d h t", d=2), bv[:, :, bass.ds(i * 2, 2), :])
                    st.settle()
                    nc.vector.tensor_scalar(ngc[:], gcp[:], -1.0, None, ALU.mult).then_inc(s_col, 1)
                    dve.wait_ge(s_col, i * 2 + 1)
                    for c in range(NC):
                        convolve(i, c, st)
                    dve.wait_ge(s_act, i * (6 + NG) + 1)
                    nc.vector.tensor_scalar(neg[:], neg[:], -1.0, None, ALU.mult).then_inc(s_col, 1)
                    dve.wait_ge(s_col, i * 2 + 2)
                    for n in range(4):
                        normalise(i, n)
                    for r in range(3):
                        for x in range(2):
                            lower(i, 2 * r + x, st)
                        for lv in range(1, LV + 1):
                            for x in range(2):
                                mask(i, r, x, lv)
                            if r:
                                scan(i, 2 * (r - 1) + (lv - 1) // 3, (lv - 1) % 3)
                            for x in range(2):
                                advance(i, r, x, lv)
                    for g in (4, 5):
                        scan(i, g, 0)
                        scan(i, g, 2)
                    dve.wait_ge(s_oc, i * NG + NG)
                    o0 = obuf[:, 0].rearrange("p t h c -> p (t h) c")
                    o1 = obuf[:, 1].rearrange("p t h c -> p (t h) c")
                    st.done(nc.vector.tensor_tensor(o0, o0, o1, ALU.add))
                    st.settle()
                    st.done(nc.vector.tensor_tensor(o1, o0, o0, ALU.mult))
                    st.settle()
                    nc.vector.tensor_reduce(oss[:], o1, AX, ALU.add).then_inc(s_oss, 1)
                    dve.wait_ge(s_z, i * 16 + 16)
                    z3 = zg[:].rearrange("p t (h c) -> p (t h) c", h=2)
                    st.done(nc.vector.tensor_tensor(o0, o0, z3, ALU.mult))
                    dve.wait_ge(s_ors, i + 1)
                    st.settle()
                    nc.vector.tensor_tensor(o0, o0, bcast(ors[:], 2, P), ALU.mult).then_inc(s_on, 1)
                    assert st.n == per, st.n

            @block.gpsimd
            def _(pool):
                pool.sem_inc(s_qd, 2)

                def mask_decay(i, g):
                    x = g % 2
                    pool.wait_ge(s_rows[x], i * 96 + (g // 2 + 1) * 32)
                    if g >= 2:
                        pool.wait_ge(s_lt, i * NG + g + 1)
                    four = dt[:, x].rearrange("p (d h) c -> p d h c", d=2)
                    nc.gpsimd.tensor_tensor(four, rows[:, x, :, 0].rearrange("p (d h) c -> p d h c", d=2), bcast(k.causal, 2, 2), ALU.add).then_inc(s_dtin, 1)

                def decay_kq(i, g):
                    x, par, tiles = g % 2, (g // 2) % 2, group_tiles(g)
                    pool.wait_ge(s_eg, i * NG + g + 1)
                    if g == 0:
                        pool.wait_ge(s_nrm, i * 4 + 4)
                        pool.wait_ge(s_kvc, i * 6 + 6)
                    if g >= 4:
                        pool.wait_ge(s_o, i * NG + g - 3)
                        pool.wait_ge(s_sn, i * n_sn + sn_at(g - 4))
                    for d in range(2):
                        t, two = tiles[d], slice(2 * d, 2 * d + 2)
                        nc.gpsimd.tensor_tensor(qd[:, par, x, two], kq[:, :, 1, t * P:(t + 1) * P], rows[:, x, two, 0], ALU.mult)
                        last = nc.gpsimd.tensor_tensor(kd[:, par, x, two], ktok[:, t], bcast(edl[:, x, two], 2, P), ALU.mult)
                    last.then_inc(s_qd, 1)

                def beta_inverse(i, g):
                    x, par, tiles, r = g % 2, (g // 2) % 2, group_tiles(g), g // 2
                    pool.wait_ge(s_tt[x], i * 21 + 7 * r + 7)
                    for d in range(2):
                        two = slice(2 * d, 2 * d + 2)
                        last = nc.gpsimd.tensor_tensor(tf[:, par, x, two], tt[:, x, two],
                                                       bcast(bcp[:, two, tiles[d]], 2, P), ALU.mult)
                    last.then_inc(s_tf, 1)

                with pool.Fori(0, HP) as i:
                    pool.wait_ge(s_col, i * 2 + 1)
                    for g in (0, 1):
                        mask_decay(i, g)
                    for r in range(3):
                        for x in range(2):
                            decay_kq(i, 2 * r + x)
                        if r < 2:
                            for x in range(2):
                                mask_decay(i, 2 * (r + 1) + x)
                        for x in range(2):
                            beta_inverse(i, 2 * r + x)
    k.gdn_ctx.close()


def output_and_route(k):
    nc, a, ps = k.nc, k.a, k.psum
    R = k.route_ctx = k.ctx.enter_context(ExitStack())
    k.idx_s = k.sb("idx_s", [CS, NE], U32, R)
    k.idx_p = k.sb("idx_p", [CP, NE], U32, R)
    k.gates = k.sb("gates", [CT, NE], F32, R)
    k.xn_p = nc.dram_tensor("xn_prompt", [SP_, D], F32).ap()
    k.xn_s = nc.dram_tensor("xn_sample", [SS_, D], F32).ap()
    GR = 4
    with ExitStack() as c:
        sb = lambda n, s, dt=F32: k.sb(n, s, dt, c)
        sem = lambda n: k.sem(n, c)
        mixT = sb("mixT", [P, 2 * H, T])
        x2 = sb("x2", [P, NT, D])
        wo = sb("wo", [P, 2, 2 * H, 512])
        junk = sb("junk_d", [P, 512])
        ssp = sb("ssp", [P, NT, GR])
        ss = sb("ss_d", [P, NT])
        rs = sb("rs_d", [P, NT])
        eps_sb = sb("eps_d", [P, 1])
        lmax = sb("lmax", [P, NT])
        lsum = sb("lsum", [P, NT])
        linv = sb("linv", [P, NT])
        aff = sb("aff", [P, NT, NE])
        wflat = wo[:, 0].rearrange("p k n -> p (k n)")
        xn = wflat[:, 0:2 * D].rearrange("p (b d) -> p b d", b=2)
        xnT = wflat[:, 2 * D:3 * D].rearrange("p (k c) -> p k c", k=KD)
        g2 = wo[:, 1].rearrange("p k n -> p (k n)")[:, 0:D]
        wr = sb("wr", [P, KD, NE])
        affT = sb("affT", [NE, T])
        left = sb("left", [NE, 2, SS_])
        vals = sb("vals", [NE, CT])
        idx = sb("idx", [NE, CT], U32)
        idxf = sb("idxf", [NE, CT])

        s_mix = [sem(f"mix_loaded{q}") for q in range(4)]
        s_x = sem("x_reloaded")
        s_w = [sem("wo_loaded0"), sem("wo_loaded1")]
        s_r = sem("router_loaded")
        s_acc = sem("output_projected")
        s_x2 = sem("residual_added")
        s_ssp = sem("residual_squared")
        s_rs = sem("rms2")
        s_xs = sem("x2_scaled")
        s_xn = sem("x2_normed")
        s_out = sem("rows_out")
        s_xno = [sem("xn_out0"), sem("xn_out1")]
        s_tp = sem("xn_transposed")
        s_tc = sem("xnT_stored")
        s_lg = sem("logits")
        s_lm = sem("logit_max")
        s_le = sem("logit_exp")
        s_af = sem("affinity")
        s_at = sem("affinity_transposed")
        s_atc = sem("affinity_stored")
        s_top = sem("top_step")
        s_sel = sem("selected")
        s_selt = sem("selected_transposed")
        s_vec = sem("route_vector_step")
        s_act = sem("route_scalar_step")

        wo_d = a["w_o"][0].rearrange("(k p) n -> p k n", p=P)

        with nc.Block() as block:
            @block.sync
            def _(sp):
                def load_w(i, j):
                    sp.dma_start(wo[:, j], wo_d[:, :, bass.ds(i * 1024 + 512 * j, 512)]).then_inc(s_w[j], 16)

                for q in range(4):
                    if q == 1:
                        load_w(0, 0)
                    sp.dma_start(mixT[:, 4 * q:4 * q + 4, :], k.mix[4 * q:4 * q + 4].rearrange("h p t -> p h t")).then_inc(s_mix[q], 16)
                sp.dma_start(x2[:, 0:TILES_P, :], a["x_prompt"][0].rearrange("(t p) d -> p t d", p=P)).then_inc(s_x, 16)
                sp.dma_start(x2[:, TILES_P:NT, :], a["x_sample"][0].rearrange("(t p) d -> p t d", p=P)).then_inc(s_x, 16)
                load_w(0, 1)
                for j in range(2):
                    sp.wait_ge(s_acc, NT * (j + 1))
                    load_w(1, j)
                sp.dma_start(wr[:], a["w_router"][0].rearrange("(p k) e -> p k e", k=KD)).then_inc(s_r, 16)
                sp.wait_ge(s_acc, NT * GR)
                sp.dma_start(g2, a["norm2_g"][0].partition_broadcast(P)).then_inc(s_r, 16)
                for t in range(NT):
                    if t == 0:
                        sp.wait_ge(s_x2, NT * GR)
                    sp.dma_start(k.y_rows(t), x2[:, t, :]).then_inc(s_out, 16)
                    sp.wait_ge(s_xn, t + 1)
                    dst = k.xn_p[t * P:(t + 1) * P] if t < TILES_P else k.xn_s[(t - TILES_P) * P:(t - TILES_P + 1) * P]
                    sp.dma_start(dst, xn[:, t % 2, :]).then_inc(s_xno[t % 2], 16)
                sp.wait_ge(s_out, 16 * NT)
                for q in s_xno:
                    sp.wait_ge(q, 16 * NT // 2)

            @block.tensor
            def _(pe):
                with pe.Fori(0, GR // 2) as i:
                    for j in range(2):
                        pe.wait_ge(s_w[j], i * 16 + 16)
                        for t in range(NT):
                            u = NT * j + t
                            pe.wait_ge(s_x2, i * (2 * NT) + u + 1)
                            for q in range(2 * H):
                                if u == 0 and q % 4 == 0:
                                    pe.wait_ge(s_mix[q // 4], 16)
                                last = nc.tensor.matmul(ps[:, u % 3, :], mixT[:, q, t * P:(t + 1) * P], wo[:, j, q, :],
                                                        start=(q == 0), stop=(q == 2 * H - 1))
                            last.then_inc(s_acc, 1)
                pe.wait_ge(s_r, 32)
                for t in range(NT):
                    pe.wait_ge(s_xn, t + 1)
                    v = xn[:, t % 2, :].rearrange("p (c k) -> p k c", k=KD)
                    for b in range(4):
                        m = 4 * t + b
                        if m >= 4:
                            pe.wait_ge(s_tc, m - 3)
                        for j in range(4):
                            last = nc.tensor.transpose(ps[:, 3 + b, j * P:(j + 1) * P], v[:, 4 * b + j, :], k.ident)
                        last.then_inc(s_tp, 1)
                    pe.wait_ge(s_tc, 4 * t + 4)
                    if t:
                        pe.wait_ge(s_le, t)
                    for q in range(KD):
                        last = nc.tensor.matmul(ps[:, 7, 0:NE], xnT[:, q, :], wr[:, q, :], start=(q == 0), stop=(q == KD - 1))
                    last.then_inc(s_lg, 1)
                    pe.wait_ge(s_af, t + 1)
                    if t:
                        pe.wait_ge(s_atc, t)
                    nc.tensor.transpose(ps[0:NE, 0, 0:P], aff[:, t, :], k.ident).then_inc(s_at, 1)
                pe.wait_ge(s_sel, 1)
                nc.tensor.transpose(ps[0:CS, 1, 0:NE], idxf[:, 0:CS], k.ident[0:NE, 0:NE])
                nc.tensor.transpose(ps[0:CP, 1, NE:2 * NE], idxf[:, CS:CT], k.ident[0:NE, 0:NE])
                nc.tensor.transpose(ps[0:CT, 1, 2 * NE:3 * NE], vals[:], k.ident[0:NE, 0:NE]).then_inc(s_selt, 1)

            @block.vector
            def _(dve):
                dve.sem_inc(s_x2, 3)
                nc.vector.memset(eps_sb[:], EPS).then_inc(s_vec, 1)
                dve.wait_ge(s_x, 32)
                with dve.Fori(0, GR // 2) as i:
                    for j in range(2):
                        for t in range(NT):
                            u = NT * j + t
                            dve.wait_ge(s_acc, i * (2 * NT) + u + 1)
                            o = x2[:, t, bass.ds(i * 1024 + 512 * j, 512)]
                            nc.vector.tensor_tensor(o, ps[:, u % 3, :], o, ALU.add).then_inc(s_x2, 1)
                st = Steps(dve, s_vec)
                st.n = 1
                dve.wait_ge(s_ssp, NT * GR)
                st.done(nc.vector.tensor_reduce(ss[:], ssp[:], AX, ALU.add))
                dve.wait_ge(s_r, 32)

                def norm(t):
                    dve.wait_ge(s_xs, t + 1)
                    nc.vector.tensor_tensor(xn[:, t % 2, :], xn[:, t % 2, :], g2, ALU.mult).then_inc(s_xn, 1)

                def store(t, b):
                    dve.wait_ge(s_tp, 4 * t + b + 1)
                    if b == 0 and t:
                        dve.wait_ge(s_lg, t)
                    nc.vector.tensor_copy(xnT[:, 4 * b:4 * b + 4, :].rearrange("p k c -> p (k c)"), ps[:, 3 + b, :]).then_inc(s_tc, 1)

                def softmax(t):
                    dve.wait_ge(s_lg, t + 1)
                    st.done(nc.vector.reduce_max(lmax[:, t:t + 1], ps[:, 7, 0:NE], AX))
                    st.settle()
                    nc.vector.tensor_scalar(lmax[:, t:t + 1], lmax[:, t:t + 1], -1.0, None, ALU.mult).then_inc(s_lm, 1)
                    dve.wait_ge(s_le, t + 1)
                    st.done(nc.vector.reciprocal(linv[:, t:t + 1], lsum[:, t:t + 1]))
                    st.settle()
                    nc.vector.tensor_scalar(aff[:, t, :], aff[:, t, :], linv[:, t:t + 1], None, ALU.mult).then_inc(s_af, 1)
                    dve.wait_ge(s_at, t + 1)
                    nc.vector.tensor_copy(affT[:, t * P:(t + 1) * P], ps[0:NE, 0, 0:P]).then_inc(s_atc, 1)

                tops = [0]

                def top(c0, S, v0, C):
                    src = affT[:, c0:c0 + S]
                    for r in range(C // 8):
                        v, o = vals[:, v0 + 8 * r:v0 + 8 * r + 8], left[:, r % 2, 0:S]
                        nc.vector.max(v, src).then_inc(s_top, 1)
                        tops[0] += 1
                        dve.wait_ge(s_top, tops[0])
                        nc.vector.max_index(idx[:, v0 + 8 * r:v0 + 8 * r + 8], v, src).then_inc(s_top, 1)
                        nc.vector.match_replace(o, v, src, -1.0).then_inc(s_top, 1)
                        tops[0] += 2
                        dve.wait_ge(s_top, tops[0])
                        src = o

                norm(0)
                for t in range(NT):
                    for b in range(4):
                        store(t, b)
                    if t + 1 < NT:
                        norm(t + 1)
                    softmax(t)
                    if t == TILES_P - 1:
                        dve.wait_ge(s_atc, TILES_P)
                        top(0, SP_, CS, CP)
                dve.wait_ge(s_atc, NT)
                top(SP_, SS_, 0, CS)
                nc.vector.tensor_copy(idxf[:], idx[:]).then_inc(s_sel, 1)
                dve.wait_ge(s_selt, 1)
                nc.vector.tensor_copy(k.idx_s[:], ps[0:CS, 1, 0:NE])
                nc.vector.tensor_copy(k.idx_p[:], ps[0:CP, 1, NE:2 * NE])
                nc.vector.tensor_copy(k.gates[:], ps[0:CT, 1, 2 * NE:3 * NE]).then_inc(s_sel, 1)

            @block.scalar
            def _(act):
                act.preload_act_table_set(TABLES)
                act.wait_ge(s_vec, 1)
                with act.Fori(0, GR // 2) as i:
                    for j in range(2):
                        for t in range(NT):
                            u = NT * j + t
                            act.wait_ge(s_x2, i * (2 * NT) + u + 4)
                            act.wait_ge(s_ssp, i * (2 * NT) + u) if u else None
                            nc.scalar.activation(junk[:], x2[:, t, bass.ds(i * 1024 + 512 * j, 512)], ACT.Square,
                                                 accum_out=ssp[:, t, bass.ds(i * 2 + j, 1)]).then_inc(s_ssp, 1)
                            if u == 2 * NT - 1:
                                act.wait_ge(s_ssp, i * (2 * NT) + 2 * NT)
                st = Steps(act, s_act)
                act.wait_ge(s_vec, 2)
                st.done(nc.scalar.activation(rs[:], ss[:], ACT.Ln, bias=eps_sb[:], scale=1.0 / D))
                st.settle()
                st.done(nc.scalar.activation(rs[:], rs[:], ACT.Exp, scale=-0.5))
                st.settle()
                act.wait_ge(s_acc, NT * GR)

                def scale(t):
                    if t >= 2:
                        act.wait_ge(s_tp, 4 * (t - 1))
                        act.wait_ge(s_xno[t % 2], 16 * (t // 2))
                    nc.scalar.activation(xn[:, t % 2, :], x2[:, t, :], ACT.Copy, scale=rs[:, t:t + 1]).then_inc(s_xs, 1)

                scale(0)
                scale(1)
                for t in range(NT):
                    act.wait_ge(s_lm, t + 1)
                    nc.scalar.activation(aff[:, t, :], ps[:, 7, 0:NE], ACT.Exp, bias=lmax[:, t:t + 1],
                                         accum_out=lsum[:, t:t + 1]).then_inc(s_le, 1)
                    if t + 2 < NT:
                        scale(t + 2)


def moe(k):
    nc, a, ps = k.nc, k.a, k.psum
    UNITS, RING = 12, 6
    with ExitStack() as c:
        sb = lambda n, s, dt=F32: k.sb(n, s, dt, c)
        sem = lambda n: k.sem(n, c)
        ring = sb("ring", [P, RING, 4096])
        xe = sb("xe", [CT, D])
        xeT = sb("xeT", [P, KD, CT])
        h = sb("h", [CT, FF])
        hT = sb("hT", [P, FF // P, CT])
        ye = sb("ye", [CT, D])
        gate = sb("gate", [CT, 1])
        gs = sb("gather_sample", [CS, 1], U32)
        gp = sb("gather_prompt", [CP, 1], U32)
        ss = sb("scatter_sample", [CS, 1], U32)
        sp = sb("scatter_prompt", [CP, 1], U32)

        s_w = [sem(f"unit_loaded{q}") for q in range(RING)]
        s_u = sem("unit_used")
        s_ix = sem("indices_ready")
        s_ga = sem("gathered")
        s_tb = sem("batch_transposed")
        s_ev = sem("batch_stored")
        s_sg = sem("gate_silu")
        s_h = sem("hidden")
        s_gc = sem("gate_column")
        s_ye = sem("expert_output")
        s_sc = sem("scattered")
        s_free = sem("expert_output_free")

        gate_d = a["w_gate"][0].rearrange("e (p k) f -> e p k f", k=KD)
        up_d = a["w_up"][0].rearrange("e (p k) f -> e p k f", k=KD)
        down_d = a["w_down"][0].rearrange("e (k p) n -> e p k n", p=P)

        with nc.Block() as block:
            @block.sync
            def _(sync):
                with sync.Fori(0, NE) as e:
                    for u in range(UNITS):
                        wait_apart(sync, s_u, e * UNITS + u + 1, k)
                        wait_apart(sync, s_w[u % RING], e * 32 + 16 * (u // RING) + 16, k)
                        q = u % 4
                        if u < 8:
                            src = (gate_d if u < 4 else up_d)[bass.ds(e, 1), :, 4 * q:4 * q + 4, :]
                            src = src.rearrange("o p k f -> (o p) (k f)")
                            sync.dma_start(ring[:, u % RING, :], src).then_inc(s_w[u % RING], 16)
                        else:
                            src = down_d[bass.ds(e, 1), :, :, 512 * q:512 * q + 512].rearrange("o p k f -> (o p) k f")
                            sync.dma_start(ring[:, u % RING, :].rearrange("p (k n) -> p k n", k=8), src).then_inc(s_w[u % RING], 16)

            @block.tensor
            def _(pe):
                pe.sem_inc(s_u, RING)
                for q in s_w:
                    pe.sem_inc(q, 16)

                def transpose_x(e):
                    first = isinstance(e, int) and e == 0
                    pe.wait_ge(s_ga, e * 32 + 32)
                    v = xe[:].rearrange("t (c k) -> t k c", k=KD)
                    for b in range(4):
                        if first and b >= 2:
                            pe.wait_ge(s_ev, b - 1)
                        elif not first:
                            pe.wait_ge(s_ev, e * 6 + b - 3)
                        for j in range(4):
                            last = nc.tensor.transpose(ps[:, 6 + b % 2, j * CT:(j + 1) * CT], v[:, 4 * b + j, :], k.ident[0:CT, 0:CT])
                        last.then_inc(s_tb, 1)

                def expert(e, more):
                    for u in range(8):
                        pe.wait_ge(s_w[u % RING], e * 32 + 16 * (u // RING) + 32)
                        if u == 0:
                            pe.wait_ge(s_ev, e * 6 + 4)
                            pe.wait_ge(s_sg, e + 1)
                        if u == 4:
                            pe.wait_ge(s_h, e + 1)
                        w = ring[:, u % RING, :].rearrange("p (k f) -> p k f", k=4)
                        for kk in range(4):
                            q = 4 * (u % 4) + kk
                            for half in range(2):
                                last = nc.tensor.matmul(ps[0:CT, 2 * (u // 4) + half, :], xeT[:, q, :], w[:, kk, 512 * half:512 * half + 512],
                                                        start=(q == 0), stop=(q == KD - 1))
                        last.then_inc(s_u, 1)
                    if more:
                        transpose_x(e + 1)
                    pe.wait_ge(s_h, e + 2)
                    for b in range(2):
                        pe.wait_ge(s_ev, e * 6 + (8 if more else 4) + b - 1)
                        for j in range(4):
                            f = 4 * b + j
                            last = nc.tensor.transpose(ps[:, 6 + b % 2, j * CT:(j + 1) * CT], h[:, f * P:(f + 1) * P], k.ident[0:CT, 0:CT])
                        last.then_inc(s_tb, 1)
                    pe.wait_ge(s_ev, e * 6 + (10 if more else 6))
                    for u in range(8, UNITS):
                        pe.wait_ge(s_w[u % RING], e * 32 + 48)
                        pe.wait_ge(s_ye, e * 4 + (u - 8) + 1)
                        w = ring[:, u % RING, :].rearrange("p (k n) -> p k n", k=8)
                        for q in range(8):
                            last = nc.tensor.matmul(ps[0:CT, 4 + u % 2, :], hT[:, q, :], w[:, q, :], start=(q == 0), stop=(q == 7))
                        last.then_inc(s_u, 1)

                transpose_x(0)
                with pe.Fori(0, NE - 1) as e:
                    expert(e, True)
                expert(NE - 1, False)

            @block.scalar
            def _(act):
                act.preload_act_table_set("silu_and_others")

                def store_x(e):
                    for b in range(4):
                        act.wait_ge(s_tb, b + 1 if isinstance(e, int) else e * 6 + b - 1)
                        nc.scalar.copy(xeT[:, 4 * b:4 * b + 4, :].rearrange("p k c -> p (k c)"), ps[:, 6 + b % 2, 0:4 * CT]).then_inc(s_ev, 1)

                def expert(e, more):
                    act.wait_ge(s_u, e * UNITS + 4 + RING)
                    act.wait_ge(s_tb, e * 6 + 4)
                    for half in range(2):
                        last = nc.scalar.activation(h[:, 512 * half:512 * half + 512], ps[0:CT, half, :], ACT.Silu)
                    last.then_inc(s_sg, 1)
                    if more:
                        store_x(e + 1)
                    for b in range(2):
                        act.wait_ge(s_tb, e * 6 + (8 if more else 4) + b + 1)
                        nc.scalar.copy(hT[:, 4 * b:4 * b + 4, :].rearrange("p k c -> p (k c)"), ps[:, 6 + b % 2, 0:4 * CT]).then_inc(s_ev, 1)

                act.sem_inc(s_sg, 1)
                store_x(0)
                with act.Fori(0, NE - 1) as e:
                    expert(e, True)
                expert(NE - 1, False)

            @block.vector
            def _(dve):
                dve.sem_inc(s_h, 1)
                dve.sem_inc(s_ye, 2)
                with dve.Fori(0, NE) as e:
                    dve.wait_ge(s_ye, e * 4 + 2)
                    nc.vector.tensor_copy(gate[:], k.gates[:, bass.ds(e, 1)]).then_inc(s_gc, 1)
                    dve.wait_ge(s_u, e * UNITS + 8 + RING)
                    dve.wait_ge(s_sg, e + 2)
                    for half in range(2):
                        x = h[:, 512 * half:512 * half + 512]
                        last = nc.vector.tensor_tensor(x, x, ps[0:CT, 2 + half, :], ALU.mult)
                    last.then_inc(s_h, 1)
                    dve.wait_ge(s_gc, e + 1)
                    dve.wait_ge(s_free, e + 1)
                    for q in range(4):
                        dve.wait_ge(s_u, e * UNITS + 9 + q + RING)
                        nc.vector.tensor_scalar(ye[:, 512 * q:512 * q + 512], ps[0:CT, 4 + q % 2, :], gate[:, 0:1], None,
                                                ALU.mult).then_inc(s_ye, 1)

            @block.gpsimd
            def _(pool):
                pool.sem_inc(s_free, 1)

                def indices(e, ixs, ixp):
                    nc.gpsimd.tensor_copy(ixs[:], k.idx_s[:, bass.ds(e, 1)])
                    nc.gpsimd.tensor_copy(ixp[:], k.idx_p[:, bass.ds(e, 1)]).then_inc(s_ix, 1)

                def gather(e):
                    if not (isinstance(e, int) and e == 0):
                        pool.wait_ge(s_ga, e * 32)
                    indices(e, gs, gp)
                    wait_apart(pool, s_ix, 1 if isinstance(e, int) else e * 2, k)
                    nc.gpsimd.indirect_dma_start(xe[0:CS, :], None, k.xn_s,
                                                 bass.IndirectOffsetOnAxis(ap=gs[:, 0:1], axis=0)).then_inc(s_ga, 16)
                    nc.gpsimd.indirect_dma_start(xe[CS:CT, :], None, k.xn_p,
                                                 bass.IndirectOffsetOnAxis(ap=gp[:, 0:1], axis=0)).then_inc(s_ga, 16)

                def scatter(e, before):
                    indices(e, ss, sp)
                    pool.wait_ge(s_ix, e * 2 + before)
                    wait_apart(pool, s_ye, e * 4 + 6, k)
                    nc.gpsimd.indirect_dma_start(a["y_sample"][0], bass.IndirectOffsetOnAxis(ap=ss[:, 0:1], axis=0),
                                                 ye[0:CS, :], None, compute_op=ALU.add).then_inc(s_sc, 16)
                    nc.gpsimd.indirect_dma_start(a["y_prompt"][0], bass.IndirectOffsetOnAxis(ap=sp[:, 0:1], axis=0),
                                                 ye[CS:CT, :], None, compute_op=ALU.add).then_inc(s_sc, 16)
                    pool.wait_ge(s_sc, e * 32 + 32)
                    pool.sem_inc(s_free, 1)

                gather(0)
                with pool.Fori(0, NE - 1) as e:
                    pool.wait_ge(s_tb, e * 6 + 4)
                    gather(e + 1)
                    scatter(e, 3)
                scatter(NE - 1, 2)


_INS = ["x_prompt", "x_sample", "norm1_g", "w_in", "q_a_norm_g", "w_q_b", "kv_a_norm_g", "w_kv_b", "q_norm_g",
        "k_norm_g", "conv_w", "a_log_fwd", "a_log_bwd", "dt_bias_fwd", "dt_bias_bwd", "gdn_norm_g", "w_o",
        "norm2_g", "w_router", "w_gate", "w_up", "w_down"]
_OUTS = {"y_prompt": (1, SP_, D), "y_sample": (1, SS_, D)}


def kernel(**inputs):
    import numpy as _np
    import concourse.bacc as _bacc
    from concourse import mybir as _mybir
    from concourse.bass_utils import run_bass_kernel_spmd as _run

    nc = _bacc.Bacc("TRN2", target_bir_lowering=False, num_devices=1)
    square, rope = shape_constants()
    arrays, a = {}, {}
    for name in _INS:
        arrays[f"in_{name}"] = _np.ascontiguousarray(inputs[name])
    arrays["in_square"], arrays["in_rope"] = square, rope
    for name, v in arrays.items():
        a[name[3:]] = nc.dram_tensor(name, v.shape, _mybir.dt.from_np(v.dtype), kind="ExternalInput").ap()
    for name, shape in _OUTS.items():
        a[name] = nc.dram_tensor(f"out_{name}", shape, F32, kind="ExternalOutput").ap()
    build(nc, a)
    r = _run(nc, [arrays], core_ids=[0])
    return tuple(r.results[0][f"out_{name}"] for name in _OUTS)
```
